# Optimizing a Trainium2 kernel written in Bass

```python
import math
import jax, jax.numpy as jnp
from jax import lax
import numpy as np

"""Hybrid conditioned decoder trunk: DEPTH post-norm (DeepNorm) residual layers.
Even layers: gated DeltaNet heads || S5 diagonal-SSM channel groups (one combined input
projection, concatenated outputs, one output projection). Odd layers: short gated conv
channels || differential-attention heads with ALiBi (same pattern). Every layer is followed
by a dense SwiGLU FFN. Every sub-layer is adaLN-modulated by a per-sequence vector c.
Inputs: x (BATCH, SEQ, D_MODEL) f32, c (BATCH, D_MODEL) f32, plus parameters.
Output: (BATCH, SEQ, D_MODEL).
"""

D_MODEL = 2048
BATCH = 1
SEQ = 256
DEPTH = 2

D_MIX = D_MODEL
N_EVEN = (DEPTH + 1) // 2
N_ODD = DEPTH // 2
A_WIDTH = D_MIX // 2
A_HEAD_DIM = 128
A_HEADS = A_WIDTH // A_HEAD_DIM
A_CONV = 4
CHUNK = 64
B_WIDTH = D_MIX - A_WIDTH
S5_GROUP = 16
S5_GROUPS = B_WIDTH // S5_GROUP
S5_STATE = 64
C_WIDTH = D_MIX // 2
C_CONV = 3
D_WIDTH = D_MIX - C_WIDTH
DA_HEAD_DIM = 128
DA_HEADS = D_WIDTH // (2 * DA_HEAD_DIM)
Q_BLOCK = 128
D_FF = ((8 * D_MODEL // 3 + 255) // 256) * 256
AB_IN = 4 * A_WIDTH + 2 * A_HEADS + B_WIDTH
CD_IN = 3 * C_WIDTH + 3 * D_WIDTH
ALPHA = (2.0 * DEPTH) ** 0.25
BETA = (8.0 * DEPTH) ** -0.25
EPS = 1e-5

kernel_name = "hybrid_deltanet_s5_shortconv_diffattn_deepnorm_adaln"

def layer_norm(x, g, b):
    xf = x.astype(jnp.float32)
    mu = jnp.mean(xf, axis=-1, keepdims=True)
    var = jnp.mean(jnp.square(xf - mu), axis=-1, keepdims=True)
    return ((xf - mu) * lax.rsqrt(var + EPS) * g + b).astype(x.dtype)

def rms_norm(x, g):
    xf = x.astype(jnp.float32)
    return xf * lax.rsqrt(jnp.mean(jnp.square(xf), axis=-1, keepdims=True) + EPS) * g

def l2_normalize(t):
    return t * lax.rsqrt(jnp.sum(jnp.square(t), axis=-1, keepdims=True) + 1e-6)

def causal_dwconv(x, w):
    K = w.shape[0]
    L = x.shape[1]
    xp = jnp.pad(x, ((0, 0), (K - 1, 0), (0, 0)))
    return sum(w[k] * xp[:, k:k + L] for k in range(K))

def chunk_gated_delta(q, k, v, g, beta):
    Bsz, H, L, dk = q.shape
    dv = v.shape[-1]
    n = L // CHUNK
    q = q.reshape(Bsz, H, n, CHUNK, dk)
    k = k.reshape(Bsz, H, n, CHUNK, dk)
    v = v.reshape(Bsz, H, n, CHUNK, dv)
    g = jnp.cumsum(g.reshape(Bsz, H, n, CHUNK), axis=-1)
    beta = beta.reshape(Bsz, H, n, CHUNK)
    tril = jnp.tril(jnp.ones((CHUNK, CHUNK), dtype=bool))
    strict = jnp.tril(jnp.ones((CHUNK, CHUNK), dtype=bool), k=-1)
    gdiff = g[..., :, None] - g[..., None, :]
    decay = jnp.where(tril, jnp.exp(jnp.where(tril, gdiff, 0.0)), 0.0)
    k_beta = k * beta[..., None]
    v_beta = v * beta[..., None]
    lower = jnp.where(strict, jnp.einsum('bhnid,bhnjd->bhnij', k_beta, k) * decay, 0.0)
    eye = jnp.eye(CHUNK, dtype=jnp.float32)
    T = lax.linalg.triangular_solve(eye + lower, jnp.broadcast_to(eye, lower.shape),
                                    left_side=True, lower=True, unit_diagonal=True)
    u = jnp.einsum('bhnij,bhnjd->bhnid', T, v_beta)
    w = jnp.einsum('bhnij,bhnjd->bhnid', T, k_beta * jnp.exp(g)[..., None])
    intra = jnp.where(tril, jnp.einsum('bhnid,bhnjd->bhnij', q, k) * decay, 0.0)
    q_decay = q * jnp.exp(g)[..., None]
    k_tail = k * jnp.exp(g[..., -1:] - g)[..., None]
    g_last = jnp.exp(g[..., -1])

    def step(S, inp):
        u_n, w_n, qd_n, a_n, kt_n, gl_n = inp
        v_new = u_n - jnp.einsum('bhik,bhkv->bhiv', w_n, S)
        o_n = jnp.einsum('bhik,bhkv->bhiv', qd_n, S) + jnp.einsum('bhij,bhjv->bhiv', a_n, v_new)
        S = S * gl_n[..., None, None] + jnp.einsum('bhik,bhiv->bhkv', kt_n, v_new)
        return S, o_n

    xs = (jnp.moveaxis(u, 2, 0), jnp.moveaxis(w, 2, 0), jnp.moveaxis(q_decay, 2, 0),
          jnp.moveaxis(intra, 2, 0), jnp.moveaxis(k_tail, 2, 0), jnp.moveaxis(g_last, 2, 0))
    S0 = jnp.zeros((Bsz, H, dk, dv), jnp.float32)
    _, o = lax.scan(step, S0, xs)
    return jnp.moveaxis(o, 0, 2).reshape(Bsz, H, L, dv)

def gated_deltanet(q, k, v, z, b, a, conv_w, a_log, dt_bias, norm_g):
    Bsz, L, _ = q.shape
    out_dtype = z.dtype
    qkv = jax.nn.silu(causal_dwconv(jnp.concatenate([q, k, v], axis=-1), conv_w)).astype(jnp.float32)
    q, k, v = jnp.split(qkv, 3, axis=-1)

    def heads(t):
        return t.reshape(Bsz, L, A_HEADS, A_HEAD_DIM).transpose(0, 2, 1, 3)

    q = l2_normalize(heads(q)) * (A_HEAD_DIM ** -0.5)
    k = l2_normalize(heads(k))
    v = heads(v)
    beta = jax.nn.sigmoid(b.astype(jnp.float32)).transpose(0, 2, 1)
    g = (-jnp.exp(a_log.astype(jnp.float32))
         * jax.nn.softplus(a.astype(jnp.float32) + dt_bias.astype(jnp.float32))).transpose(0, 2, 1)
    o = chunk_gated_delta(q, k, v, g, beta).transpose(0, 2, 1, 3)
    zh = z.astype(jnp.float32).reshape(Bsz, L, A_HEADS, A_HEAD_DIM)
    o = rms_norm(o, norm_g) * jax.nn.silu(zh)
    return o.reshape(Bsz, L, A_WIDTH).astype(out_dtype)

def _ssm_combine(left, right):
    a_l, b_l = left
    a_r, b_r = right
    return a_r * a_l, a_r * b_l + b_r

def s5_ssm(u, a_re, a_im, b_re, b_im, c_re, c_im, d, log_dt, w_glu):
    Bsz, L, _ = u.shape
    uf = u.astype(jnp.float32).reshape(Bsz, L, S5_GROUPS, S5_GROUP)
    lam = lax.complex(a_re.astype(jnp.float32), a_im.astype(jnp.float32))
    delta = jnp.exp(log_dt.astype(jnp.float32))[:, None]
    a_bar = jnp.exp(lam * delta)
    b_mat = lax.complex(b_re.astype(jnp.float32), b_im.astype(jnp.float32))
    b_bar = ((a_bar - 1.0) / lam)[:, :, None] * b_mat
    c_mat = lax.complex(c_re.astype(jnp.float32), c_im.astype(jnp.float32))
    bu = jnp.einsum('gpc,blgc->blgp', b_bar, uf.astype(jnp.complex64))
    a_seq = jnp.broadcast_to(a_bar, bu.shape)
    _, states = lax.associative_scan(_ssm_combine, (a_seq, bu), axis=1)
    y = jnp.einsum('gcp,blgp->blgc', c_mat, states).real + d.astype(jnp.float32) * uf
    y = jax.nn.gelu(y).reshape(Bsz, L, B_WIDTH)
    y = y * jax.nn.sigmoid(y @ w_glu.astype(jnp.float32))
    return y.astype(u.dtype)

def diff_attention(q, k, v, lq1, lk1, lq2, lk2, norm_g, lambda_init):
    Bsz, L, _ = q.shape
    out_dtype = v.dtype
    q = q.astype(jnp.float32).reshape(Bsz, L, DA_HEADS, 2, DA_HEAD_DIM).transpose(0, 2, 3, 1, 4)
    k = k.astype(jnp.float32).reshape(Bsz, L, DA_HEADS, 2, DA_HEAD_DIM).transpose(0, 2, 3, 1, 4)
    v = v.astype(jnp.float32).reshape(Bsz, L, DA_HEADS, 2 * DA_HEAD_DIM).transpose(0, 2, 1, 3)
    lam = (jnp.exp(jnp.sum(lq1.astype(jnp.float32) * lk1.astype(jnp.float32)))
           - jnp.exp(jnp.sum(lq2.astype(jnp.float32) * lk2.astype(jnp.float32))) + lambda_init)
    scale = DA_HEAD_DIM ** -0.5
    slopes = 2.0 ** (-8.0 * jnp.arange(1, DA_HEADS + 1, dtype=jnp.float32) / DA_HEADS)
    nb = L // Q_BLOCK
    q_blocks = jnp.moveaxis(q.reshape(Bsz, DA_HEADS, 2, nb, Q_BLOCK, DA_HEAD_DIM), 3, 0)
    kpos = jnp.arange(L)

    def one_block(args):
        qb, bi = args
        qpos = bi * Q_BLOCK + jnp.arange(Q_BLOCK)
        dist = qpos[:, None] - kpos[None, :]
        bias = -slopes[:, None, None] * dist.astype(jnp.float32)
        s = jnp.einsum('bhiqd,bhikd->bhiqk', qb, k) * scale + bias[None, :, None]
        s = jnp.where(dist >= 0, s, -jnp.inf)
        p = jax.nn.softmax(s, axis=-1)
        attn = p[:, :, 0] - lam * p[:, :, 1]
        return jnp.einsum('bhqk,bhkv->bhqv', attn, v)

    o = lax.map(one_block, (q_blocks, jnp.arange(nb)))
    o = jnp.moveaxis(o, 0, 2).reshape(Bsz, DA_HEADS, L, 2 * DA_HEAD_DIM)
    o = rms_norm(o, norm_g) * (1.0 - lambda_init)
    return o.transpose(0, 2, 1, 3).reshape(Bsz, L, D_WIDTH).astype(out_dtype)

def mixer_ab(h, w_in, w_out, conv_w, a_log, dt_bias, norm_g,
             a_re, a_im, b_re, b_im, c_re, c_im, d, log_dt, w_glu):
    proj = h @ w_in
    offs = [A_WIDTH, 2 * A_WIDTH, 3 * A_WIDTH, 4 * A_WIDTH,
            4 * A_WIDTH + A_HEADS, 4 * A_WIDTH + 2 * A_HEADS]
    q, k, v, z, b, a, u = jnp.split(proj, offs, axis=-1)
    ya = gated_deltanet(q, k, v, z, b, a, conv_w, a_log, dt_bias, norm_g)
    yb = s5_ssm(u, a_re, a_im, b_re, b_im, c_re, c_im, d, log_dt, w_glu)
    return jnp.concatenate([ya, yb], axis=-1) @ w_out

def mixer_cd(h, w_in, w_out, conv_w, lq1, lk1, lq2, lk2, norm_g, lambda_init):
    proj = h @ w_in
    offs = [C_WIDTH, 2 * C_WIDTH, 3 * C_WIDTH, 3 * C_WIDTH + D_WIDTH, 3 * C_WIDTH + 2 * D_WIDTH]
    gb, gc, xc, q, k, v = jnp.split(proj, offs, axis=-1)
    yc = gb * causal_dwconv(gc * xc, conv_w)
    yd = diff_attention(q, k, v, lq1, lk1, lq2, lk2, norm_g, lambda_init)
    return jnp.concatenate([yc, yd], axis=-1) @ w_out

def swiglu(h, w_gate, w_up, w_down):
    return (jax.nn.silu(h @ w_gate) * (h @ w_up)) @ w_down

def setup_inputs(seed: int = 0) -> dict:
    key = jax.random.key(seed)
    ks = iter(jax.random.split(key, 48))
    nrm = lambda shape, s: jax.random.normal(next(ks), shape, jnp.float32) * s
    inp = {}
    inp["x"] = nrm((BATCH, SEQ, D_MODEL), 1.0)
    inp["c"] = nrm((BATCH, D_MODEL), 1.0)
    inp["ada_w"] = nrm((DEPTH, D_MODEL, 6 * D_MODEL), 0.1 * D_MODEL ** -0.5)
    inp["ada_b"] = nrm((DEPTH, 6 * D_MODEL), 0.01)
    inp["ln1_g"] = 1.0 + nrm((DEPTH, D_MODEL), 0.02)
    inp["ln1_b"] = nrm((DEPTH, D_MODEL), 0.02)
    inp["ln2_g"] = 1.0 + nrm((DEPTH, D_MODEL), 0.02)
    inp["ln2_b"] = nrm((DEPTH, D_MODEL), 0.02)
    inp["ffn_w_gate"] = nrm((DEPTH, D_MODEL, D_FF), D_MODEL ** -0.5)
    inp["ffn_w_up"] = nrm((DEPTH, D_MODEL, D_FF), D_MODEL ** -0.5)
    inp["ffn_w_down"] = nrm((DEPTH, D_FF, D_MODEL), BETA * D_FF ** -0.5)
    inp["ab_w_in"] = nrm((N_EVEN, D_MODEL, AB_IN), D_MODEL ** -0.5)
    inp["ab_w_out"] = nrm((N_EVEN, D_MIX, D_MODEL), BETA * D_MIX ** -0.5)
    inp["dn_conv_w"] = nrm((N_EVEN, A_CONV, 3 * A_WIDTH), A_CONV ** -0.5)
    inp["dn_a_log"] = jnp.log(jax.random.uniform(next(ks), (N_EVEN, A_HEADS), jnp.float32, 1.0, 16.0))
    dt = jnp.exp(jax.random.uniform(next(ks), (N_EVEN, A_HEADS), jnp.float32,
                                    math.log(1e-3), math.log(1e-1)))
    inp["dn_dt_bias"] = dt + jnp.log(-jnp.expm1(-dt))
    inp["dn_norm_g"] = 1.0 + nrm((N_EVEN, A_HEAD_DIM), 0.02)
    inp["s5_a_re"] = -0.5 + nrm((N_EVEN, S5_GROUPS, S5_STATE), 0.01)
    inp["s5_a_im"] = math.pi * jnp.arange(S5_STATE, dtype=jnp.float32) + nrm((N_EVEN, S5_GROUPS, S5_STATE), 0.01)
    inp["s5_b_re"] = nrm((N_EVEN, S5_GROUPS, S5_STATE, S5_GROUP), (2 * S5_GROUP) ** -0.5)
    inp["s5_b_im"] = nrm((N_EVEN, S5_GROUPS, S5_STATE, S5_GROUP), (2 * S5_GROUP) ** -0.5)
    inp["s5_c_re"] = nrm((N_EVEN, S5_GROUPS, S5_GROUP, S5_STATE), 0.5)
    inp["s5_c_im"] = nrm((N_EVEN, S5_GROUPS, S5_GROUP, S5_STATE), 0.5)
    inp["s5_d"] = nrm((N_EVEN, S5_GROUPS, S5_GROUP), 1.0)
    inp["s5_log_dt"] = jax.random.uniform(next(ks), (N_EVEN, S5_GROUPS), jnp.float32,
                                          math.log(1e-3), math.log(1e-1))
    inp["s5_w_glu"] = nrm((N_EVEN, B_WIDTH, B_WIDTH), B_WIDTH ** -0.5)
    inp["cd_w_in"] = nrm((N_ODD, D_MODEL, CD_IN), D_MODEL ** -0.5)
    inp["cd_w_out"] = nrm((N_ODD, D_MIX, D_MODEL), BETA * D_MIX ** -0.5)
    inp["sc_conv_w"] = nrm((N_ODD, C_CONV, C_WIDTH), C_CONV ** -0.5)
    inp["da_lq1"] = nrm((N_ODD, DA_HEAD_DIM), 0.1)
    inp["da_lk1"] = nrm((N_ODD, DA_HEAD_DIM), 0.1)
    inp["da_lq2"] = nrm((N_ODD, DA_HEAD_DIM), 0.1)
    inp["da_lk2"] = nrm((N_ODD, DA_HEAD_DIM), 0.1)
    inp["da_norm_g"] = 1.0 + nrm((N_ODD, 2 * DA_HEAD_DIM), 0.02)
    return inp

def reference(x, c, ada_w, ada_b, ln1_g, ln1_b, ln2_g, ln2_b, ffn_w_gate, ffn_w_up, ffn_w_down,
              ab_w_in, ab_w_out, dn_conv_w, dn_a_log, dn_dt_bias, dn_norm_g,
              s5_a_re, s5_a_im, s5_b_re, s5_b_im, s5_c_re, s5_c_im, s5_d, s5_log_dt, s5_w_glu,
              cd_w_in, cd_w_out, sc_conv_w, da_lq1, da_lk1, da_lq2, da_lk2, da_norm_g):
    c_act = jax.nn.silu(c)
    for i in range(DEPTH):
        mod = c_act @ ada_w[i] + ada_b[i]
        sh1, sc1, g1, sh2, sc2, g2 = [m[:, None, :] for m in jnp.split(mod, 6, axis=-1)]
        h = x * (1.0 + sc1) + sh1
        j = i // 2
        if i % 2 == 0:
            y = mixer_ab(h, ab_w_in[j], ab_w_out[j], dn_conv_w[j], dn_a_log[j], dn_dt_bias[j],
                         dn_norm_g[j], s5_a_re[j], s5_a_im[j], s5_b_re[j], s5_b_im[j],
                         s5_c_re[j], s5_c_im[j], s5_d[j], s5_log_dt[j], s5_w_glu[j])
        else:
            lambda_init = 0.8 - 0.6 * math.exp(-0.3 * i)
            y = mixer_cd(h, cd_w_in[j], cd_w_out[j], sc_conv_w[j], da_lq1[j], da_lk1[j],
                         da_lq2[j], da_lk2[j], da_norm_g[j], lambda_init)
        x = layer_norm(ALPHA * x + (1.0 + g1) * y, ln1_g[i], ln1_b[i])
        h = x * (1.0 + sc2) + sh2
        y = swiglu(h, ffn_w_gate[i], ffn_w_up[i], ffn_w_down[i])
        x = layer_norm(ALPHA * x + (1.0 + g2) * y, ln2_g[i], ln2_b[i])
    return x


_drawn_inputs = setup_inputs


def setup_inputs(seed=0):
    import zlib

    import numpy as np

    out = dict(_drawn_inputs(seed))
    spreads = {}
    factors = {'ada_b': 4.558,
     'dn_norm_g': 8.0,
     's5_a_re': 200.0,
     'da_lk1': 3.417,
     'da_lq2': 5.012,
     'da_lk2': 8.0,
     'da_norm_g': 84.888,
     's5_a_im': 34.032,
     's5_b_re': 46.896,
     's5_b_im': 46.76,
     's5_c_re': 46.0,
     's5_c_im': 46.136,
     's5_log_dt': 37.648}
    for name, (base, spread) in spreads.items():
        noise = np.random.default_rng([zlib.crc32(name.encode()), seed]).standard_normal(out[name].shape)
        drawn = base * np.exp(spread * noise) if base else spread * noise
        out[name] = __import__('jax').numpy.asarray(drawn.astype(out[name].dtype))
    for name, factor in factors.items():
        out[name] = (out[name] * factor).astype(out[name].dtype)
    return out
```

```python
import math
from contextlib import ExitStack

import concourse.bass as bass
from concourse import mybir

F32 = mybir.dt.float32
F32R = mybir.dt.float32r
ALU = mybir.AluOpType
ACT = mybir.ActivationFunctionType
AX_X = mybir.AxisListType.X

P = 128
D = 2048
L = 256
DEPTH = 2
KT = D // P
D_FF = ((8 * D // 3 + 255) // 256) * 256
HALF = D // 2
HT = HALF // P
ALPHA = (2.0 * DEPTH) ** 0.25
EPS = 1e-5
LAMBDA_INIT = 0.8 - 0.6 * math.exp(-0.3)
DA_HEADS = HALF // (2 * P)
S5_TILES = 64 * 64 // P
GROUP = 512
GT = GROUP // P
UK = 4
ROUND_1 = 1.5 * 2.0 ** 23
BIG = -1.0e30
N_ADA = 6 * KT
FFN_BLOCKS = [(0, 4), (4, 4), (8, 3)]
AB_SMALL = 4 * HALF
N_SMALL = 2 * HT
LEVELS = 7

ADA_FIRST = 5
TWO_PI_LOW = 6.283185
N_VEC_LOADS, N_PAR_LOADS = 19, 7

ADA_AT = {0: [0] * 12, 1: [1, 1, 0, 1, 1, 0, 0, 0, 0, 0, 0, 0], 2: [1, 1, 1, 1, 1, 1, 2, 0]}
ADA_SUM = {0: {}, 1: {6: 0}, 2: {4: 0, 7: 1}}
ADA_TAKE = {0: {}, 1: {7: 0}, 2: {5: 0, 7: 1}}


class Steps:

    def __init__(self, semaphore, names, start=0):
        self.sem, self.names, self.n, self.start = semaphore, names.split(), len(names.split()), start

    def at(self, i, name):
        return i * self.n + (self.names.index(name) + 1 + self.start)

    def begin(self, i):
        return i * self.n + self.start


def plan(w):
    products = []

    def add(name, bodies, groups, units, k0=0, ada=0):
        products.append(dict(name=name, bodies=bodies, groups=groups, units=units, k0=k0, ada=ada))

    def ffn(layer, ada_up, ada_down):
        g, u, d = w["gate"][layer], w["up"][layer], w["down"][layer]
        for n, (first, groups) in enumerate(FFN_BLOCKS):
            add(f"up{layer}{n}", groups, [(g, first * GROUP, GROUP), (u, first * GROUP, GROUP)], 4, ada=ada_up)
            if groups == 4:
                add(f"down{layer}{n}", 2, [(d, 0, 2 * GROUP), (d, GROUP, 2 * GROUP)], 4, k0=first * GT, ada=ada_down)
            else:
                add(f"down{layer}{n}", 1, [(d, j * GROUP, 0) for j in range(4)], groups, k0=first * GT, ada=ada_down)

    pair = [(0, 2), (1, 2)]
    u_col = AB_SMALL + N_SMALL
    add("in0u", 1, [(w["in0"], u_col + GROUP * a, 0) for a, _ in pair], 4, ada=2)
    add("in0", 4, [(w["in0"], GROUP * a, 2 * GROUP) for a, _ in pair], 4, ada=0)
    add("glu", 1, [(w["glu"], GROUP * a, 0) for a, _ in pair], 2)
    products[-1]["ada_after"] = 2 * HT // 2
    add("out0", 2, [(w["out0"], GROUP * a, 2 * GROUP) for a, _ in pair], 4, ada=2)
    ffn(0, 1, 1)
    add("in1", 6, [(w["in1"], GROUP * a, 2 * GROUP) for a, _ in pair], 4, ada=1)
    add("out1", 2, [(w["out1"], GROUP * a, 2 * GROUP) for a, _ in pair], 4, ada=1)
    ffn(1, 0, 0)
    u = g = 0
    ab = 2 * ADA_FIRST
    for p in products:
        p.update(u0=u, g0=g, ab0=ab, bu=p["units"] * len(p["groups"]), bg=len(p["groups"]))
        u += p["bodies"] * p["bu"]
        g += p["bodies"] * p["bg"]
        ab += p["bodies"] * p["ada"]
        p["ab1"] = ab
        ab += p.get("ada_after", 0)
        assert u % 4 == 0 and g % 2 == 0
    assert ab == 2 * N_ADA // GT, ab
    return products, u


def build(nc, x, c, ada_w, ada_b, ln1_g, ln1_b, ln2_g, ln2_b, ffn_w_gate, ffn_w_up, ffn_w_down,
          ab_w_in, ab_w_out, dn_conv_w, dn_a_log, dn_dt_bias, dn_norm_g,
          s5_a_re, s5_a_im, s5_b_re, s5_b_im, s5_c_re, s5_c_im, s5_d, s5_log_dt, s5_w_glu,
          cd_w_in, cd_w_out, sc_conv_w, da_lq1, da_lk1, da_lq2, da_lk2, da_norm_g, out):
    products, n_units = plan(dict(
        gate=[ffn_w_gate[i] for i in range(DEPTH)], up=[ffn_w_up[i] for i in range(DEPTH)],
        down=[ffn_w_down[i] for i in range(DEPTH)], in0=ab_w_in[0], glu=s5_w_glu[0], out0=ab_w_out[0],
        in1=cd_w_in[0], out1=cd_w_out[0]))
    by_name = {p["name"]: p for p in products}

    ctx = ExitStack()
    with ctx:
        def sb(name, shape, dt=F32):
            return ctx.enter_context(nc.sbuf_tensor(name, shape, dt))

        def sem(name):
            return ctx.enter_context(nc.semaphore(name))

        def shared(layout):
            with ExitStack() as s:
                return [s.enter_context(nc.sbuf_tensor(n, shape, F32 if not dt else dt[0])) for n, shape, *dt in layout]

        raw = sb("w_raw", [P, 4, UK, GROUP])
        whi = sb("w_hi", [P, 2, UK, GROUP], F32R)
        wlo = sb("w_lo", [P, 2, UK, GROUP], F32R)
        aw = sb("ada_units", [P, 2, UK, GROUP])
        acc = sb("ada_acc", [P, 2, GROUP])
        xT = sb("xT", [P, KT, L])
        ahi = sb("act_hi", [P, KT, L], F32R)
        alo = sb("act_lo", [P, KT, L], F32R)
        mod = sb("mod", [P, DEPTH * N_ADA])
        adab = sb("ada_b_cols", [P, DEPTH * N_ADA])
        lnc = sb("ln_cols", [P, 4 * DEPTH * KT])
        dcw = sb("dn_conv_cols", [P, 4 * 3 * HT])
        misc = sb("misc_cols", [P, 64])
        ident = sb("ident", [P, P])
        ones = sb("ones", [P, P])
        cact = sb("c_act", [P, KT])
        onep = sb("one_plus", [P, 2, KT])
        pidle = sb("pool_idle", [P, 2])
        consts = sb("consts", [P, 8])
        s5c = sb("s5_cols", [P, 3 * S5_TILES])
        wba = sb("w_small", [P, KT, N_SMALL])
        ba = sb("ba", [P, 2, N_SMALL])
        dnb = sb("dn_small", [P, 2, HT])

        y, hhi, hlo, gt, gs, st = shared([("y", [P, KT, L]), ("hid_hi", [P, 16, L], F32R), ("hid_lo", [P, 16, L], F32R),
                                      ("gate_t", [P, GT, L]), ("gate_s", [P, GT, L]),
                                          ("ln_stat", [P, 2, L])])
        xrow, vrow = shared([("x_rows", [P, 2, D]), ("vec_rows", [P, 7, P])])
        (orow,) = shared([("out_rows", [P, 2, D])])
        (pr, s5br, s5bi, s5cr, s5ci, s5mk, s5mt, s5pad, s5w, s5tab, s5arg, s5m1, s5m2, s5z, s5v, tcol) = shared([
            ("proj0", [P, 5 * HT, L]),
            ("s5_b_re_t", [P, S5_TILES, 16]), ("s5_b_im_t", [P, S5_TILES, 16]),
            ("s5_c_re_t", [P, HT, 64]), ("s5_c_im_t", [P, HT, 64]),
            ("s5_mask", [P, 4, P]), ("s5_mask_t", [P, 4, P]),
            ("s5_pad", [P, 4, P]), ("s5_w", [P, 4, P]), ("s5_tab", [P, 3, L]), ("s5_arg", [P, 2, L]),
            ("s5_m1", [P, 2, L]), ("s5_m2", [P, 2, L]), ("s5_z", [P, 2, L]),
            ("s5_vec", [P, 3, S5_TILES]), ("s5_time", [P, L])])
        (pp, at, vn, sst, kt, _, lm, tri, dng, cv, sq, m, mb, d, dt, vt, rr) = shared([
            ("dn_p", [P, 4, P]), ("dn_at", [P, 4, P]), ("dn_vnew", [P, 4, P]), ("dn_state", [P, 2, P]),
            ("dn_ktok", [P, 2, P]), ("dn_proj0", [P, 4 * HT, L]), ("dn_levels", [P, LEVELS, P]),
            ("dn_tri", [P, P]), ("dn_gates", [P, 10, 2, HT]), ("dn_conv", [P, 6, L]), ("dn_sq", [P, 2, L]),
            ("dn_m", [P, 4, P]), ("dn_mb", [P, 4, P]), ("dn_d", [P, 4, P]), ("dn_dt", [P, 4, P]),
            ("dn_vtok", [P, 4, P]), ("dn_r", [P, 4, P])])
        (pr1, scm, scv, daq, dand, das, dae, dac, dact, davt, dao, dav) = shared([
            ("proj1", [P, 6 * HT, L]), ("sc_m", [P, 2, L]), ("sc_conv", [P, 2, L]), ("da_q", [P, 2, L]),
            ("da_nd", [P, 3 * P]), ("da_s", [P, 2, L]), ("da_e", [P, 2, L]),
            ("da_c", [P, L]), ("da_ct", [P, 3, P]), ("da_vtok", [P, 2, L]), ("da_o", [P, 2, L]),
            ("da_vec", [P, 48])])
        pg = ctx.enter_context(nc.psum_tensor("groups", [P, 2, GT, L], F32))
        pgf = pg[:].rearrange("p a (b c) t -> p (a b) (c t)", b=2)
        pm, pa, pb, pc = [ctx.enter_context(nc.psum_tensor(n, [P, 512], F32)) for n in ("pm", "pa", "pb", "pc")]

        raw_in = [sem(f"raw_in{i}") for i in range(4)]
        ada_in = [sem(f"ada_in{i}") for i in range(2)]
        hi_done, lo_done = sem("hi_done"), sem("lo_done")
        tile_used = sem("tile_used")
        grp_done = sem("grp_done")
        gate_t, hid_hi, hid_lo = sem("gate_t"), sem("hid_hi"), sem("hid_lo")
        ada_step = sem("ada_step")
        ada_summed, mod_taken = sem("ada_summed"), sem("mod_taken")
        vec_in, x_in, par_in, vec_fix = sem("vec_in"), sem("x_in"), sem("par_in"), sem("vec_fix")
        const_done, vec_turned, vec_taken = sem("const_done"), sem("vec_turned"), sem("vec_taken")
        x_turned, x_taken, c_tanh, c_done = sem("x_turned"), sem("x_taken"), sem("c_tanh"), sem("c_done")
        h_ready, h_hi, act_ready = sem("h_ready"), sem("h_hi"), sem("act_ready")
        glu_t, glu_s, glu_hi = sem("glu_t"), sem("glu_s"), sem("glu_hi")
        chain, pool_chain, pool_c = sem("dve_chain"), sem("pool_chain"), sem("pool_const")
        pool_links = [0]
        ln_r, ln_sum, ln_mean, ln_c, ln_sq = sem("ln_r"), sem("ln_sum"), sem("ln_mean"), sem("ln_c"), sem("ln_sq")
        ln_var, ln_std, ln_n, ln_gb = sem("ln_var"), sem("ln_std"), sem("ln_n"), sem("ln_gb")
        o_turned, o_taken, out_done = sem("o_turned"), sem("o_taken"), sem("out_done")

        s5_set = Steps(sem("s5_set_act"), "delta tanh sins")
        s5_setd = Steps(sem("s5_set_dve"), "x f done")
        s5_setp = Steps(sem("s5_set_pool"), "masks")
        s5p = Steps(sem("s5_pool"), "turns whole sine over cosine pad")
        s5_turned, s5_bu, s5_y = sem("s5_turned"), sem("s5_bu"), sem("s5_y")
        s5a = Steps(sem("s5_act"), "wb tab0 tab1 tab2 wc wneg")
        s5d = Steps(sem("s5_dve"), "m1 m2a m2b z sr si p1 p2")
        s5ga = Steps(sem("s5_gelu_act"), "th")
        s5_hi, s5_lo = sem("s5_hi"), sem("s5_lo")
        s5gd = Steps(sem("s5_gelu_dve"), "yv y2 p q s ys", start=1)
        ba_done, ba_taken = sem("ba_done"), sem("ba_taken")

        dna_set = Steps(sem("dn_set_act"), "tanh ealog eabs ln eG tail0")
        dnd_set = Steps(sem("dn_set_dve"), "pre g arg done")
        dne_set = Steps(sem("dn_set_pe"), "cum")
        dnp_set = Steps(sem("dn_set_pool"), "tri masks")
        dnd = Steps(sem("dn_dve"), "c0 c1 c2 c3 sl0 sl1 sl2 rq nq rk nk gt bt dm m0 m1 am r0 "
                    + " ".join(f"dt{k}" for k in range(LEVELS)) + " r1a r1 o1 rmsr on zs yz lo", start=1)
        dna = Steps(sem("dn_act"), "th0 th1 th2 sqq sqk stq stk zt ed vt kt "
                    + " ".join(f"p{k} d{k}" for k in range(LEVELS - 1)) + f" p{LEVELS - 1} vn0 S vn1 oc ss rs hi", start=1)
        dne = Steps(sem("dn_pe"), "nq nk gram gi bi vt kt "
                    + " ".join(f"p{k} x{k} d{k}" for k in range(LEVELS - 1))
                    + " p{0} x{0} vn0 S kS vn1 ov qS turn".format(LEVELS - 1), start=1)
        dnp = Steps(sem("dn_pool"), "init " + " ".join(f"mb{k}" for k in range(LEVELS)) + " at", start=1)

        scd = Steps(sem("sc_dve"), "m c0 c1 c2 g hi lo", start=1)
        da_setp, da_setd = Steps(sem("da_set_pool"), "nd"), Steps(sem("da_set_dve"), "prod lam")
        da_sete, da_seta = Steps(sem("da_set_pe"), "sum"), Steps(sem("da_set_act"), "exp")
        dad = Steps(sem("da_dve"), "q v s0 mx0 ng0 r0 rl0 t0 c0 s1 mx1 ng1 r1 rl1 t1 c1 rr on og hi lo", start=1)
        daa = Steps(sem("da_act"), "vt e0 ct0 e1 ct1 o sq std", start=1)
        dae_ = Steps(sem("da_pe"), "sc0 sc1 vt ct0 pv0 ct1 pv1 ss", start=1)

        VECS = [(adab[:, 0:96], pa, 0, 96), (adab[:, 96:192], pa, 96, 96), (lnc[:], pa, 192, 128), (dcw[:], pa, 320, 96),
                (misc[:, 0:55], pb, 0, 55), (s5c[:], pb, 128, 96)]
        sv = s5m1[:].rearrange("p a l -> p (a l)").rearrange("p (k t) -> p k t", t=S5_TILES)

        def along(cols, n=L):
            return cols.unsqueeze(2).broadcast_to([cols.shape[0], cols.shape[1], n])

        def over(rows, k):
            return rows.unsqueeze(1).broadcast_to([rows.shape[0], k, rows.shape[1]])

        BETA, GDEC, GCUM, EG, BEG, TAIL, EALOG, XA, SUMSQ, EABS = range(10)
        glu_end = by_name["glu"]["g0"] + 4
        pair_v = lambda buf: buf[:].rearrange("p (a c) l -> p a (c l)", c=2)
        prob_v = lambda buf: buf[:].rearrange("p (a c) l -> p a c l", c=2)

        def gate_col(row, chunk, head):
            return dng[:, row, chunk, bass.ds(head, 1)]

        def q4(bank, p):
            return bank[:, P * p:P * p + P]

        def deltanet_act(act):
            act.wait_ge(grp_done, glu_end)
            act.activation(dng[:, BETA], ba[:, :, 0:HT], ACT.Tanh, scale=0.5).then_inc(dna_set.sem, 1)
            act.activation(dng[:, EALOG, 0], dnb[:, 0], ACT.Exp).then_inc(dna_set.sem, 1)
            act.wait_ge(dnd_set.sem, dnd_set.at(0, "pre"))
            act.activation(dng[:, EABS], dng[:, EABS], ACT.Exp, scale=-1.0).then_inc(dna_set.sem, 1)
            act.wait_ge(dna_set.sem, dna_set.at(0, "eabs"))
            act.activation(dng[:, EABS], dng[:, EABS], ACT.Ln, bias=consts[:, 4:5]).then_inc(dna_set.sem, 1)
            act.wait_ge(dnd_set.sem, dnd_set.at(0, "arg"))
            act.activation(dng[:, EG], dng[:, GCUM], ACT.Exp).then_inc(dna_set.sem, 1)
            act.activation(dng[:, TAIL], dng[:, TAIL], ACT.Exp).then_inc(dna_set.sem, 1)

            with act.Fori(0, HT // 2) as i:
                def done(ins):
                    ins.then_inc(dna.sem, 1)

                def on(steps, name):
                    act.wait_ge(steps.sem, steps.at(i, name))

                on(dnd, "c3")
                done(act.activation(sq[:], cv[:, 0:2], ACT.Tanh, scale=0.5))
                done(act.activation(pair_v(d), cv[:, 2:4], ACT.Tanh, scale=0.5))
                done(act.activation(pair_v(dt), cv[:, 4:6], ACT.Tanh, scale=0.5))
                on(dnd, "sl1")
                done(act.activation(sq[:], cv[:, 0:2], ACT.Square))
                done(act.activation(pair_v(mb), cv[:, 2:4], ACT.Square))
                on(dne, "nq")
                done(act.activation(sq[:], pa[:].rearrange("p (a l) -> p a l", a=2), ACT.Sqrt, scale=0.25, bias=consts[:, 3:4]))
                on(dne, "nk")
                done(act.activation(pair_v(mb), pb[:].rearrange("p (a l) -> p a l", a=2), ACT.Sqrt, scale=0.25, bias=consts[:, 3:4]))
                on(dnd, "nk")
                done(act.activation(sq[:], pr[:, bass.ds(4 * HT + 2 * i, 2)], ACT.Tanh, scale=0.5))
                on(dnd, "dm")
                done(act.activation(pp[:], dt[:], ACT.Exp))
                on(dne, "vt")
                done(act.activation(vt[:], pgf[:, 2].rearrange("p (q l) -> p q l", q=4), ACT.Copy, scale=0.5))
                on(dne, "kt")
                act.activation(kt[:, 0], q4(pgf[:, 3], 0), ACT.Copy, scale=gate_col(TAIL, 0, 2 * i))
                done(act.activation(kt[:, 1], q4(pgf[:, 3], 1), ACT.Copy, scale=gate_col(TAIL, 0, 2 * i + 1)))
                for k in range(LEVELS):
                    on(dne, f"p{k}")
                    if k == 0:
                        on(dnd, "am")
                    done(act.activation(pp[:], pa[:].rearrange("p (q l) -> p q l", q=4), ACT.Copy))
                    if k < LEVELS - 1:
                        on(dne, f"d{k}")
                        done(act.activation(d[:], pc[:].rearrange("p (q l) -> p q l", q=4), ACT.Copy))
                on(dne, "vn0")
                done(act.activation(prob_v(vn)[:, :, 0], pgf[:, 0, 0:2 * P].rearrange("p (a l) -> p a l", a=2), ACT.Copy))
                on(dne, "S")
                done(act.activation(sst[:], pgf[:, 1, 0:2 * P].rearrange("p (a l) -> p a l", a=2), ACT.Copy))
                on(dne, "vn1")
                done(act.activation(prob_v(vn)[:, :, 1], pgf[:, 3, 0:2 * P].rearrange("p (a l) -> p a l", a=2), ACT.Copy))
                on(dne, "ov")
                done(act.activation(pp[:], pa[:].rearrange("p (q l) -> p q l", q=4), ACT.Copy))
                on(dnd, "o1")
                for p in range(4):
                    last = act.activation(vt[:, p], pp[:, p], ACT.Square, accum_out=dng[:, SUMSQ, 0, p:p + 1])
                done(last)
                act.wait_ge(dna.sem, dna.at(i, "ss"))
                done(act.activation(dng[:, SUMSQ, 0, 0:4], dng[:, SUMSQ, 0, 0:4], ACT.Sqrt, scale=1.0 / P, bias=consts[:, 0:1]))
                on(dnd, "yz")
                done(act.activation(ahi[:, bass.ds(2 * i, 2)], sq[:], ACT.Copy, scale=0.5))

        def deltanet_dve(dve, link, ada_unit, ada_take):
            dve.wait_ge(grp_done, glu_end)
            dve.wait_ge(dna_set.sem, dna_set.at(0, "ealog"))
            link(dve.tensor_scalar(dng[:, BETA], dng[:, BETA], 0.5, 0.5, ALU.mult, ALU.add))
            link(dve.tensor_tensor(dng[:, XA], ba[:, :, HT:2 * HT], over(dnb[:, 1], 2), ALU.add))
            dve.scalar_tensor_tensor(dng[:, EABS], dng[:, XA], -1.0, dng[:, XA], ALU.mult, ALU.max).then_inc(dnd_set.sem, 1)
            dve.wait_ge(dna_set.sem, dna_set.at(0, "ln"))
            link(dve.scalar_tensor_tensor(dng[:, XA], dng[:, XA], 0.0, dng[:, EABS], ALU.max, ALU.add))
            dve.scalar_tensor_tensor(dng[:, GDEC], dng[:, XA], -1.0, over(dng[:, EALOG, 0], 2), ALU.mult,
                                     ALU.mult).then_inc(dnd_set.sem, 1)
            dve.wait_ge(dne_set.sem, 1)
            link(dve.tensor_copy(dng[:, GCUM], pb[:, 0:2 * HT].rearrange("p (c h) -> p c h", c=2)))
            dve.tensor_tensor(dng[:, TAIL], pb[:, 2 * HT:4 * HT].rearrange("p (c h) -> p c h", c=2), dng[:, GCUM],
                              ALU.subtract).then_inc(dnd_set.sem, 1)
            dve.wait_ge(dna_set.sem, dna_set.at(0, "eG"))
            dve.tensor_tensor(dng[:, BEG], dng[:, BETA], dng[:, EG], ALU.mult).then_inc(dnd_set.sem, 1)
            dve.wait_ge(dnd_set.sem, dnd_set.at(0, "done"))

            with dve.Fori(0, HT // 2) as i:
                def done(ins):
                    ins.then_inc(dnd.sem, 1)

                def on(steps, name):
                    dve.wait_ge(steps.sem, steps.at(i, name))

                for other in (dna, dne, dnp):
                    dve.wait_ge(other.sem, other.begin(i))
                for tap in range(4):
                    if tap:
                        on(dnd, f"c{tap - 1}")
                    for mm in range(3):
                        for a in range(2):
                            src = pr[:, bass.ds(HT * (mm + 1) + a + 2 * i, 1)]
                            w = dcw[:, bass.ds(3 * HT * (3 - tap) + HT * mm + a + 2 * i, 1)]
                            dst = cv[:, 2 * mm + a:2 * mm + a + 1]
                            if tap == 0:
                                last = dve.tensor_scalar(dst, src, w, None, ALU.mult)
                            else:
                                last = dve.scalar_tensor_tensor(dst[:, :, tap:], src[:, :, 0:L - tap], w, dst[:, :, tap:],
                                                                ALU.mult, ALU.add)
                    done(last)
                for mm, th in enumerate((sq[:], pair_v(d), pair_v(dt))):
                    on(dna, f"th{mm}")
                    v = cv[:, 2 * mm:2 * mm + 2]
                    done(dve.scalar_tensor_tensor(v, th, 1.0, v, ALU.add, ALU.mult))
                on(dna, "stq")
                done(dve.reciprocal(sq[:], sq[:]))
                on(dnd, "rq")
                done(dve.scalar_tensor_tensor(cv[:, 0:2], cv[:, 0:2], 0.5 * P ** -0.5, sq[:], ALU.mult, ALU.mult))
                on(dna, "stk")
                done(dve.reciprocal(mb[:], mb[:]))
                on(dnd, "rk")
                done(dve.scalar_tensor_tensor(cv[:, 2:4], cv[:, 2:4], 0.5, pair_v(mb), ALU.mult, ALU.mult))
                dve.wait_ge(dnp_set.sem, 1)
                for p in range(4):
                    last = dve.tensor_scalar(rr[:, p], tri[:], gate_col(GDEC, p % 2, 2 * i + p // 2), None, ALU.mult)
                done(last)
                for p in range(4):
                    last = dve.tensor_scalar(vt[:, p], ident[:], gate_col(BETA, p % 2, 2 * i + p // 2), None, ALU.mult)
                done(last)
                on(dne, "gi")
                for p in range(4):
                    last = dve.tensor_scalar(dt[:, p], q4(pc, p), gate_col(GCUM, p % 2, 2 * i + p // 2), 0.0,
                                             ALU.subtract, ALU.min)
                done(last)
                on(dna, "ed")
                on(dne, "gram")
                v4 = lambda bank: bank.rearrange("p (q l) -> p q l", q=4)
                done(dve.tensor_tensor(m[:], v4(pgf[:, 0]), pp[:], ALU.mult))
                on(dne, "bi")
                on(dnd, "m0")
                done(dve.scalar_tensor_tensor(m[:], m[:], -1.0, v4(pb[:]), ALU.mult, ALU.mult))
                done(dve.tensor_tensor(at[:], v4(pgf[:, 1]), pp[:], ALU.mult))
                on(dna, "vt")
                for p in range(4):
                    last = dve.tensor_scalar(rr[:, p], vt[:, p], gate_col(BETA, p % 2, 2 * i + p // 2), None, ALU.mult)
                done(last)
                ab = by_name["glu"]["ab1"] + 2 * i
                for k in range(LEVELS):
                    ada_unit(ab + k // 4, k % 4, k // 4)
                    on(dnp, "init")
                    on(dne, f"x{k}")
                    done(dve.tensor_tensor(dt[:], dt[:], v4(pb[:]), ALU.add))
                ada_unit(ab + 1, 3, 1)
                on(dne, "kS")
                for a in range(2):
                    last = dve.tensor_scalar(vt[:, 2 * a], q4(pgf[:, 2], a), gate_col(BEG, 1, 2 * i + a), None, ALU.mult)
                done(last)
                on(dnd, "r1a")
                done(dve.tensor_tensor(prob_v(rr)[:, :, 1], prob_v(rr)[:, :, 1], prob_v(vt)[:, :, 0], ALU.subtract))
                ada_take(ab)
                on(dna, "oc")
                on(dne, "qS")
                for a in range(2):
                    last = dve.scalar_tensor_tensor(pp[:, 2 * a + 1], q4(pb, a), gate_col(EG, 1, 2 * i + a), pp[:, 2 * a + 1],
                                                    ALU.mult, ALU.add)
                done(last)
                on(dna, "rs")
                done(dve.reciprocal(dng[:, SUMSQ, 0, 0:4], dng[:, SUMSQ, 0, 0:4]))
                on(dnd, "rmsr")
                for p in range(4):
                    last = dve.tensor_scalar(pp[:, p], pp[:, p], dng[:, SUMSQ, 0, p:p + 1], None, ALU.mult)
                done(last)
                z = pr[:, bass.ds(4 * HT + 2 * i, 2)]
                done(dve.scalar_tensor_tensor(sq[:], sq[:], 1.0, z, ALU.add, ALU.mult))
                ada_take(ab + 1)
                on(dne, "turn")
                on(dnd, "zs")
                done(dve.scalar_tensor_tensor(sq[:], pc[:].rearrange("p (a l) -> p a l", a=2), misc[:, 48:49], sq[:],
                                              ALU.mult, ALU.mult))
                on(dna, "hi")
                done(dve.scalar_tensor_tensor(alo[:, bass.ds(2 * i, 2)], sq[:], 0.5, ahi[:, bass.ds(2 * i, 2)].bitcast(F32),
                                              ALU.mult, ALU.subtract))

        def deltanet_pe(pe, ada_sum):
            pe.wait_ge(dnp_set.sem, 1)
            pe.wait_ge(dnd_set.sem, dnd_set.at(0, "g"))
            for n, w in enumerate((tri, ones)):
                for chunk in range(2):
                    last = pe.matmul(pb[:, HT * (2 * n + chunk):HT * (2 * n + chunk + 1)], w[:], dng[:, GDEC, chunk],
                                     start=True, stop=True)
            last.then_inc(dne_set.sem, 1)
            pe.wait_ge(dnd_set.sem, dnd_set.at(0, "arg"))

            with pe.Fori(0, HT // 2) as i:
                def done(ins):
                    ins.then_inc(dne.sem, 1)

                def on(steps, name):
                    pe.wait_ge(steps.sem, steps.at(i, name))

                def each(bank, pairs):
                    for n, (a, b) in enumerate(pairs):
                        last = pe.matmul(q4(bank, n), a, b, start=True, stop=True)
                    done(last)

                def turn(bank, sources):
                    for n, a in enumerate(sources):
                        last = pe.transpose(q4(bank, n), a, ident[:])
                    done(last)

                def part(tile, chunk):
                    return cv[:, tile, P * chunk:P * chunk + P]

                problems = [(p // 2, p % 2) for p in range(4)]
                on(dna, "sqq")
                done(pe.matmul(pa[:], ones[:], sq[:], start=True, stop=True))
                on(dna, "sqk")
                done(pe.matmul(pb[:], ones[:], mb[:], start=True, stop=True))
                on(dnd, "nk")
                for n, (a, chunk) in enumerate(problems):
                    pe.matmul(q4(pgf[:, 0], n), part(2 + a, chunk), part(2 + a, chunk), start=True, stop=True)
                each(pgf[:, 1], [(part(2 + a, chunk), part(a, chunk)) for a, chunk in problems])
                on(dnd, "gt")
                done(pe.matmul(pc[:], ones[:], rr[:], start=True, stop=True))
                on(dnd, "bt")
                done(pe.matmul(pb[:], ones[:], vt[:], start=True, stop=True))
                turn(pgf[:, 2], [part(4 + a, chunk) for a, chunk in problems])
                turn(pgf[:, 3], [part(2 + a, 0) for a in range(2)])
                on(dnp, "init")
                for k in range(LEVELS):
                    on(dnp, f"mb{k}")
                    if k:
                        on(dna, f"d{k - 1}")
                    each(pa, [(mb[:, p], d[:, p]) for p in range(4)])
                    on(dna, f"p{k}")
                    if k == 0:
                        on(dnd, "m1")
                    each(pb, [(pp[:, p], dt[:, p]) for p in range(4)])
                    on(dnd, f"dt{k}")
                    if k < LEVELS - 1:
                        turn(pc, [dt[:, p] for p in range(4)])
                on(dnd, "r0")
                on(dna, "kt")
                each(pgf[:, 0], [(dt[:, 2 * a], rr[:, 2 * a]) for a in range(2)])
                on(dna, "vn0")
                on(dnd, "am")
                each(pgf[:, 1], [(kt[:, a], vn[:, 2 * a]) for a in range(2)])
                on(dna, "S")
                each(pgf[:, 2], [(part(2 + a, 1), sst[:, a]) for a in range(2)])
                on(dnd, "r1")
                each(pgf[:, 3], [(dt[:, 2 * a + 1], rr[:, 2 * a + 1]) for a in range(2)])
                ada_sum(by_name["glu"]["ab1"] + 2 * i, 0)
                on(dna, "vn1")
                on(dnp, "at")
                each(pa, [(at[:, p], vn[:, p]) for p in range(4)])
                each(pb, [(part(a, 1), sst[:, a]) for a in range(2)])
                ada_sum(by_name["glu"]["ab1"] + 2 * i + 1, 1)
                on(dnd, "on")
                turn(pc, [pp[:, p] for p in range(4)])

        def deltanet_pool(pool):
            pool.wait_ge(grp_done, glu_end)
            pool.memset(tri[:], 1.0)
            link_pool(pool, pool.memset(lm[:], 0.0))
            link_pool(pool, pool.affine_select(out=tri[:], in_=tri[:], compare_op=ALU.is_ge, fill=0.0, base=0,
                                               pattern=[[1, P]], channel_multiplier=-1))
            for k in range(LEVELS):
                size = 1 << k
                v = lm[:, k].rearrange("p (n h s) -> p n h s", h=2, s=size)[:, :, 1]
                link_pool(pool, pool.affine_select(out=v, in_=v, compare_op=ALU.is_gt, fill=1.0, base=0,
                                                   pattern=[[2 * size, P // (2 * size)], [0, size]], channel_multiplier=-1))
                link_pool(pool, pool.affine_select(out=v, in_=v, compare_op=ALU.is_gt, fill=0.0, base=size,
                                                   pattern=[[2 * size, P // (2 * size)], [0, size]], channel_multiplier=-1))
            pool.sem_inc(dnp_set.sem, 1)
            with pool.Fori(0, HT // 2) as i:
                def done(ins):
                    ins.then_inc(dnp.sem, 1)

                def on(steps, name):
                    pool.wait_ge(steps.sem, steps.at(i, name))

                on(dna, "ed")
                carry(pool)
                pool.tensor_copy(d[:], ident[:].unsqueeze(1).broadcast_to([P, 4, P]))
                done(pool.tensor_copy(dt[:], ident[:].unsqueeze(1).broadcast_to([P, 4, P])))
                on(dnd, "m1")
                for k in range(LEVELS):
                    if k:
                        on(dne, f"p{k - 1}")
                    done(pool.tensor_tensor(mb[:], m[:], lm[:, k].unsqueeze(1).broadcast_to([P, 4, P]), ALU.mult))
                on(dnd, "am")
                done(pool.tensor_tensor(at[:], at[:], tri[:].unsqueeze(1).broadcast_to([P, 4, P]), ALU.mult))

        GB, GC, XC, Q, K, V = (HT * n for n in range(6))
        SLOPE, MAXES, SUMS, NEGLAM, LAMS = 0, 4, 8, 12, 13
        MQ = 51

        def attention_act(act):
            act.wait_ge(da_sete.sem, 1)
            act.activation(dav[:, LAMS:LAMS + 2], pm[:, 0:2], ACT.Exp).then_inc(da_seta.sem, 1)
            with act.Fori(0, DA_HEADS) as h:
                def done(ins):
                    ins.then_inc(daa.sem, 1)

                def on(steps, name):
                    act.wait_ge(steps.sem, steps.at(h, name))

                on(dae_, "vt")
                done(act.activation(davt[:].rearrange("p a l -> p (a l)"), pgf[:, 2], ACT.Copy))
                for b in range(2):
                    w = P * (b + 1)
                    on(dad, f"ng{b}")
                    for mp in range(2):
                        last = act.activation(das[:, mp, 0:w], das[:, mp, 0:w], ACT.Exp,
                                              bias=dav[:, MAXES + mp:MAXES + mp + 1],
                                              accum_out=dav[:, SUMS + mp:SUMS + mp + 1])
                    done(last)
                    on(dae_, f"ct{b}")
                    done(act.activation(dact[:, b:2 * b + 1].rearrange("p k l -> p (k l)"),
                                        pgf[:, 3, P * b:P * b + w], ACT.Copy))
                on(dae_, "pv1")
                done(act.activation(dao[:].rearrange("p a l -> p (a l)"), pa[:], ACT.Copy))
                done(act.activation(das[:].rearrange("p a l -> p (a l)"), pa[:], ACT.Square))
                on(dae_, "ss")
                done(act.activation(dac[:], pb[:, 0:L], ACT.Sqrt, scale=1.0 / (2 * P), bias=consts[:, 0:1]))

        def attention_dve(dve):
            last_group = by_name["in1"]["g0"] + 12 + 2
            dve.wait_ge(grp_done, last_group)
            with dve.Fori(0, HT) as t:
                def step(ins, then=None):
                    ins.then_inc(scd.sem, 1)
                    if then:
                        dve.wait_ge(scd.sem, scd.at(t, then))

                dve.wait_ge(scd.sem, scd.begin(t))
                mm, cc = scm[:, 0:1], scv[:, 0:1]
                step(dve.tensor_tensor(mm, pr1[:, bass.ds(GC + t, 1)], pr1[:, bass.ds(XC + t, 1)], ALU.mult), "m")
                step(dve.tensor_scalar(cc, mm, misc[:, bass.ds(16 + 2 * HT + t, 1)], None, ALU.mult), "c0")
                for tap in (1, 2):
                    step(dve.scalar_tensor_tensor(cc[:, :, tap:], mm[:, :, 0:L - tap],
                                                  misc[:, bass.ds(16 + (2 - tap) * HT + t, 1)], cc[:, :, tap:],
                                                  ALU.mult, ALU.add), f"c{tap}")
                step(dve.tensor_tensor(cc, cc, pr1[:, bass.ds(GB + t, 1)], ALU.mult), "g")
                step(dve.tensor_copy(ahi[:, bass.ds(t, 1)], cc), "hi")
                step(dve.tensor_tensor(alo[:, bass.ds(t, 1)], cc, ahi[:, bass.ds(t, 1)].bitcast(F32), ALU.subtract))
            dve.tensor_tensor(dav[:, LAMS:LAMS + 2], misc[:, MQ:MQ + 3:2], misc[:, MQ + 1:MQ + 4:2],
                              ALU.mult).then_inc(da_setd.sem, 1)
            dve.wait_ge(da_seta.sem, 1)
            dve.scalar_tensor_tensor(dav[:, NEGLAM:NEGLAM + 1], dav[:, LAMS + 1:LAMS + 2], -LAMBDA_INIT, dav[:, LAMS:LAMS + 1],
                                     ALU.add, ALU.subtract).then_inc(da_setd.sem, 1)
            dve.wait_ge(da_setd.sem, da_setd.at(0, "lam"))
            dve.wait_ge(da_setp.sem, 1)
            with dve.Fori(0, DA_HEADS) as h:
                def done(ins):
                    ins.then_inc(dad.sem, 1)

                def on(steps, name):
                    dve.wait_ge(steps.sem, steps.at(h, name))

                for other in (daa, dae_):
                    dve.wait_ge(other.sem, other.begin(h))
                dve.wait_ge(dad.sem, dad.begin(h))
                done(dve.tensor_scalar(daq[:], pr1[:, bass.ds(Q + 2 * h, 2)], P ** -0.5, None, ALU.mult))
                done(dve.tensor_copy(dao[:], pr1[:, bass.ds(V + 2 * h, 2)]))
                for b in range(2):
                    w = P * (b + 1)
                    on(dae_, f"sc{b}")
                    if b:
                        on(dad, "c0")
                    dist = dand[:, P * b:P * b + w].unsqueeze(1).broadcast_to([P, 2, w])
                    done(dve.scalar_tensor_tensor(das[:, :, 0:w], dist, dav[:, bass.ds(SLOPE + h, 1)],
                                                  pgf[:, b].rearrange("p (m l) -> p m l", m=2)[:, :, 0:w],
                                                  ALU.mult, ALU.add))
                    on(dad, f"s{b}")
                    done(dve.tensor_reduce(dav[:, MAXES:MAXES + 2], das[:, :, 0:w], AX_X, ALU.max))
                    on(dad, f"mx{b}")
                    done(dve.tensor_scalar(dav[:, MAXES:MAXES + 2], dav[:, MAXES:MAXES + 2], -1.0, None, ALU.mult))
                    on(daa, f"e{b}")
                    done(dve.reciprocal(dav[:, SUMS:SUMS + 2], dav[:, SUMS:SUMS + 2]))
                    on(dad, f"r{b}")
                    done(dve.tensor_tensor(dav[:, SUMS + 1:SUMS + 2], dav[:, SUMS + 1:SUMS + 2],
                                           dav[:, NEGLAM:NEGLAM + 1], ALU.mult))
                    on(dad, f"rl{b}")
                    if b:
                        on(dae_, "ct0")
                    done(dve.tensor_scalar(dac[:, 0:w], das[:, 1, 0:w], dav[:, SUMS + 1:SUMS + 2], None, ALU.mult))
                    on(dad, f"t{b}")
                    done(dve.scalar_tensor_tensor(dac[:, 0:w], das[:, 0, 0:w], dav[:, SUMS:SUMS + 1], dac[:, 0:w],
                                                  ALU.mult, ALU.add))
                on(daa, "std")
                done(dve.reciprocal(dac[:], dac[:]))
                on(dad, "rr")
                done(dve.tensor_tensor(dao[:], dao[:], over(dac[:], 2), ALU.mult))
                on(dad, "on")
                for f in range(2):
                    last = dve.tensor_scalar(dao[:, f], dao[:, f], misc[:, 49 + f:50 + f], 1.0 - LAMBDA_INIT,
                                             ALU.mult, ALU.mult)
                done(last)
                on(dad, "og")
                where = bass.ds(HT + 2 * h, 2)
                done(dve.tensor_copy(ahi[:, where], dao[:]))
                on(dad, "hi")
                done(dve.tensor_tensor(alo[:, where], dao[:], ahi[:, where].bitcast(F32), ALU.subtract))

        def attention_pe(pe):
            pe.wait_ge(grp_done, by_name["in1"]["g0"] + 12 + 2)
            pe.wait_ge(da_setd.sem, da_setd.at(0, "prod"))
            pe.matmul(pm[:, 0:2], ones[:], dav[:, LAMS:LAMS + 2], start=True, stop=True).then_inc(da_sete.sem, 1)
            with pe.Fori(0, DA_HEADS) as h:
                def done(ins):
                    ins.then_inc(dae_.sem, 1)

                def on(steps, name):
                    pe.wait_ge(steps.sem, steps.at(h, name))

                on(dad, "q")
                for b in range(2):
                    w = P * (b + 1)
                    for mp in range(2):
                        last = pe.matmul(pgf[:, b, L * mp:L * mp + w], daq[:, mp, P * b:P * b + P],
                                         pr1[:, bass.ds(K + 2 * h + mp, 1), 0:w], start=True, stop=True)
                    done(last)
                on(dad, "v")
                for chunk in range(2):
                    for f in range(2):
                        last = pe.transpose(q4(pgf[:, 2], 2 * chunk + f), dao[:, f, P * chunk:P * chunk + P], ident[:])
                done(last)
                for b in range(2):
                    on(dad, f"c{b}")
                    for n in range(b + 1):
                        last = pe.transpose(q4(pgf[:, 3], b + n), dac[:, P * n:P * n + P], ident[:])
                    done(last)
                    on(daa, f"ct{b}")
                    for f in range(2):
                        for n in range(b + 1):
                            last = pe.matmul(pa[:, L * f + P * b:L * f + P * b + P], davt[:, n, P * f:P * f + P],
                                             dact[:, b + n], start=(n == 0), stop=(n == b))
                    done(last)
                on(daa, "sq")
                for f in range(2):
                    last = pe.matmul(pb[:, 0:L], ones[:], das[:, f], start=(f == 0), stop=(f == 1))
                done(last)

        def attention_pool(pool):
            pool.wait_ge(act_ready, 12)
            pool.iota(dand[:, 0:P], [[1, P]], base=0, channel_multiplier=-1, allow_small_or_imprecise_dtypes=True)
            link_pool(pool, pool.iota(dand[:, P:3 * P], [[1, L]], base=-P, channel_multiplier=-1,
                                      allow_small_or_imprecise_dtypes=True))
            for h in range(DA_HEADS):
                pool.memset(dav[:, SLOPE + h:SLOPE + h + 1], 2.0 ** (-8.0 * (h + 1) / DA_HEADS))
            pool.affine_select(out=dand[:, 0:P], in_=dand[:, 0:P], compare_op=ALU.is_ge, fill=BIG, base=0,
                               pattern=[[-1, P]], channel_multiplier=1)
            pool.affine_select(out=dand[:, P:3 * P], in_=dand[:, P:3 * P], compare_op=ALU.is_ge, fill=BIG, base=P,
                               pattern=[[-1, L]], channel_multiplier=1).then_inc(da_setp.sem, 1)

        def link_pool(pool, ins):
            pool_links[0] += 1
            ins.then_inc(pool_chain, 1)
            pool.wait_ge(pool_chain, pool_links[0])

        def carry(pool):
            pool.tensor_tensor(pidle[:, 1:2], pidle[:, 0:1], pidle[:, 0:1], ALU.add)

        block = ctx.enter_context(nc.Block())

        def bodies(engine, n, body, peel=False):
            if n == 1:
                body(0)
            elif peel:
                with engine.Fori(0, n - 1) as i:
                    body(i)
                body(n - 1)
            else:
                with engine.Fori(0, n) as i:
                    body(i)

        def ada_source(ab0):
            layer = min(ab0 // (N_ADA // GT), DEPTH - 1)
            return ada_w[layer], (ab0 - layer * (N_ADA // GT)) * GROUP

        def mod_cols(n):
            base = n * 3 * KT
            return base, base + KT, base + 2 * KT, 12 * n + 8, 12 * n + 12

        @block.sync
        def _(sp):
            def load(dst, src, s):
                sp.dma_start(dst, src).then_inc(s, 16)

            def ada_unit(src, col, ab, j):
                sp.wait_ge(ada_step, 16 * ab + (4 * j + 1))
                sp.dma_start(aw[:, j % 2], src[UK * P * j:UK * P * (j + 1), bass.ds(col, GROUP)]
                             .rearrange("(k p) n -> p k n", p=P)).then_inc(ada_in[j % 2], 16)

            for layer in range(DEPTH):
                load(vrow[0:N_ADA, layer], ada_b[layer].rearrange("(t p) -> t p", p=P), vec_in)
            for n, v in enumerate((ln1_g, ln1_b, ln2_g, ln2_b)):
                load(vrow[32 * n:32 * n + 32, 2], v.rearrange("l (t p) -> (l t) p", p=P), vec_in)
            load(vrow[0:96, 3], dn_conv_w[0].rearrange("k (t p) -> (k t) p", p=P), vec_in)
            load(vrow[0:16, 4], c[0].rearrange("(t p) -> t p", p=P), vec_in)
            load(vrow[16:40, 4], sc_conv_w[0].rearrange("k (t p) -> (k t) p", p=P), vec_in)
            load(vrow[40:48, 4], s5_d[0].rearrange("(t g) c -> t (g c)", t=HT), vec_in)
            load(vrow[48:49, 4], dn_norm_g, vec_in)
            load(vrow[49:51, 4], da_norm_g.rearrange("a (t p) -> (a t) p", p=P), vec_in)
            for n, v in enumerate((da_lq1, da_lk1, da_lq2, da_lk2)):
                load(vrow[51 + n:52 + n, 4], v, vec_in)
            load(vrow[0:32, 5], s5_a_re[0].rearrange("(t g) s -> t (g s)", g=2), vec_in)
            load(vrow[32:64, 5], s5_a_im[0].rearrange("(t g) s -> t (g s)", g=2), vec_in)
            load(vrow[64:96, 6, 0:2], s5_log_dt[0].rearrange("(t g) -> t g", g=2), vec_in)
            load(xrow[:], x[0].rearrange("(t p) d -> p t d", p=P), x_in)
            load(wba[:], ab_w_in[0][:, AB_SMALL:AB_SMALL + N_SMALL].rearrange("(k p) n -> p k n", p=P), par_in)
            load(dnb[:, 0], dn_a_log.broadcast_to([P, HT]), par_in)
            load(dnb[:, 1], dn_dt_bias.broadcast_to([P, HT]), par_in)
            for dst, src in ((s5br, s5_b_re), (s5bi, s5_b_im)):
                load(dst[:], src[0].rearrange("(t g) s c -> (g s) t c", g=2), par_in)
            for dst, src in ((s5cr, s5_c_re), (s5ci, s5_c_im)):
                load(dst[:], src[0].rearrange("(t g) c s -> (g c) t s", t=HT), par_in)

            def ada_first(i):
                for b in range(2):
                    for j in range(4):
                        ada_unit(ada_w[0], GROUP * (2 * i + b), 2 * i + b, j)

            bodies(sp, ADA_FIRST, ada_first)

            def weight_unit(p, i, j):
                w, first, step = p["groups"][j // p["units"]]
                k = (p["k0"] + UK * (j % p["units"])) * P
                sp.wait_ge(lo_done, p["u0"] + j + p["bu"] * i + 1)
                sp.dma_start(raw[:, j % 4], w[k:k + UK * P, bass.ds(first + step * i, GROUP)]
                             .rearrange("(k p) n -> p k n", p=P)).then_inc(raw_in[j % 4], 16)

            for p in products:
                def body(i, p=p, ahead=0):
                    taken = 0
                    src, col0 = ada_source(p["ab0"])
                    for j in range(p["bu"]):
                        if j >= ahead:
                            weight_unit(p, i, j)
                        for _ in range(ADA_AT[p["ada"]][j]):
                            b, q = taken // 4, taken % 4
                            ab = p["ab0"] + b + p["ada"] * i
                            ada_unit(src, col0 + GROUP * b + GROUP * p["ada"] * i, ab, q)
                            taken += 1
                if p["name"] == "out0":
                    for j in range(4):
                        weight_unit(p, 0, j)
                    ab1 = by_name["glu"]["ab1"]
                    src, col0 = ada_source(ab1)

                    def ada_round(i):
                        for n in range(8):
                            b, q = n // 4, n % 4
                            ada_unit(src, col0 + GROUP * b + 2 * GROUP * i, ab1 + b + 2 * i, q)
                    bodies(sp, HT // 2, ada_round)
                    body(0, ahead=4)
                    body(1)
                else:
                    bodies(sp, p["bodies"], body)

            for b in range(2):
                sp.wait_ge(o_taken, 4 * b + 4)
                sp.dma_start(out[0, b * P:(b + 1) * P, :], orow[:, b]).then_inc(out_done, 16)
            sp.wait_ge(out_done, 32)

        @block.scalar
        def _(act):
            def split_hi(u4, j):
                act.activation(whi[:, j % 2], raw[:, (j + 2) % 4], ACT.Copy).then_inc(hi_done, 1)

            def product(p, evacuate, before=None, after=None):
                def body(i):
                    for j in range(p["bu"]):
                        u = p["u0"] + p["bu"] * i + j
                        static = p["bodies"] == 1
                        if before:
                            before(i, j)
                        if not (static and u + 2 >= n_units):
                            act.wait_ge(raw_in[(j + 2) % 4], 16 * ((j + 2) // 4 + 1) + (16 * (p["u0"] // 4))
                                        + 16 * (p["bu"] // 4) * i)
                            act.wait_ge(tile_used, u + 1)
                            split_hi(None, j)
                        if (j + 1) % p["units"] == 0:
                            evacuate(i, j // p["units"], u + 1)
                        if after:
                            after(i, j)
                bodies(act, p["bodies"], body, peel=before is not None)

            def take(dst):
                def evacuate(i, g, units):
                    act.wait_ge(tile_used, units)
                    act.activation(dst(i, g), pg[:, g % 2], ACT.Copy).then_inc(grp_done, 1)
                return evacuate

            def ffn(layer):
                hids = 4 * 0
                for n, (first, groups) in enumerate(FFN_BLOCKS):
                    p = by_name[f"up{layer}{n}"]

                    def up(i, g, units, p=p, done=11 * layer + first):
                        if g == 0:
                            act.wait_ge(tile_used, units)
                            act.wait_ge(grp_done, p["g0"] + 2 * i + 2)
                            act.activation(gt[:], pg[:, 0], ACT.Tanh, scale=0.5).then_inc(gate_t, 1)
                        else:
                            act.wait_ge(grp_done, p["g0"] + 2 * i + 2 + 2)
                            act.activation(hhi[:, bass.ds(GT * i, GT)], gs[:], ACT.Copy).then_inc(hid_hi, 1)
                    product(p, up)
                    p = by_name[f"down{layer}{n}"]
                    if n == 0:
                        product(p, take(lambda i, g: y[:, bass.ds(2 * GT * i + GT * g, GT)]))
                    else:
                        product(p, lambda i, g, units: None)

            def modulate(n):
                for q in range(4):
                    act.wait_ge(h_ready, 4 * n + q + 1)
                    act.activation(ahi[:, 4 * q:4 * q + 4], y[:, 4 * q:4 * q + 4], ACT.Copy).then_inc(h_hi, 1)

            def layer_norm(n):
                act.wait_ge(ln_sum, n + 1)
                act.activation(st[:, 0], pa[:, 0:L], ACT.Copy, scale=1.0 / D).then_inc(ln_mean, 1)
                for q in range(4):
                    act.wait_ge(ln_c, 4 * n + q + 1)
                    act.activation(y[:, 4 * q:4 * q + 4], xT[:, 4 * q:4 * q + 4], ACT.Square).then_inc(ln_sq, 1)
                act.wait_ge(ln_var, n + 1)
                act.activation(st[:, 1], pb[:, 0:L], ACT.Sqrt, scale=1.0 / D, bias=consts[:, 0:1]).then_inc(ln_std, 1)
                for q in range(4):
                    act.wait_ge(ln_n, 4 * n + q + 1)
                    for t in range(4 * q, 4 * q + 4):
                        g = (n % 2) * 2 * 32 + (n // 2) * KT + t
                        last = act.activation(xT[:, t], xT[:, t], ACT.Identity, scale=lnc[:, g:g + 1],
                                              bias=lnc[:, g + 32:g + 33])
                    last.then_inc(ln_gb, 1)
                    if n < 3:
                        act.wait_ge(h_ready, 4 * (n + 1) + q + 1)
                        act.activation(ahi[:, 4 * q:4 * q + 4], y[:, 4 * q:4 * q + 4], ACT.Copy).then_inc(h_hi, 1)

            for steps in (dna, daa):
                act.sem_inc(steps.sem, steps.start)
            act.wait_ge(vec_taken, 6)
            act.activation(cact[:], misc[:, 0:KT], ACT.Tanh, scale=0.5).then_inc(c_tanh, 1)
            act.activation(sv[:, 0], s5c[:, 64:96], ACT.Exp).then_inc(s5_set.sem, 1)
            act.wait_ge(s5_setd.sem, s5_setd.at(0, "x"))
            act.activation(sv[:, 2], sv[:, 1], ACT.Tanh, scale=0.5).then_inc(s5_set.sem, 1)
            act.wait_ge(s5_setd.sem, s5_setd.at(0, "f"))
            act.activation(sv[:, 5], sv[:, 4], ACT.Sin, scale=TWO_PI_LOW)
            act.activation(sv[:, 6], sv[:, 4], ACT.Sin, scale=TWO_PI_LOW / 2).then_inc(s5_set.sem, 1)

            for j in (0, 1):
                act.wait_ge(raw_in[j], 16)
                act.activation(whi[:, j], raw[:, j], ACT.Copy).then_inc(hi_done, 1)
            modulate(0)
            product(by_name["in0u"], take(lambda i, g: pr[:, GT * g:GT * g + GT]))
            act.sem_inc(s5a.sem, s5a.n)

            def s5_input_weights(n):
                act.wait_ge(s5_turned, n + 2)
                act.wait_ge(s5_bu, n + 1)
                act.activation(s5w[:, 0:2], pa[:, 0:2 * P], ACT.Copy).then_inc(s5a.sem, 1)

            def s5_tables(n):
                act.wait_ge(s5p.sem, s5p.at(n + 1, "cosine"))
                act.wait_ge(s5d.sem, s5d.at(n, "p2"))
                act.activation(s5tab[:, 0], s5arg[:, 0], ACT.Sin, scale=TWO_PI_LOW)
                act.activation(s5tab[:, 1], s5arg[:, 1], ACT.Sin, scale=TWO_PI_LOW, bias=consts[:, 1:2])
                act.activation(s5tab[:, 2], s5arg[:, 0], ACT.Sin, scale=-TWO_PI_LOW).then_inc(s5a.sem, 3)

            def s5_output_weights(n):
                act.wait_ge(s5_y, n + 1)
                act.activation(s5w[:, 2], pa[:, 2 * P:3 * P], ACT.Copy).then_inc(s5a.sem, 1)
                act.activation(s5w[:, 3], pa[:, 3 * P:4 * P], ACT.Copy, scale=-1.0).then_inc(s5a.sem, 1)

            def s5_before(i, j):
                n = 8 * i + j + 1
                last = isinstance(n, int) and n == S5_TILES
                if not last:
                    s5_input_weights(n)
                    s5_tables(n)
                if j % 4 == 3:
                    t = 2 * i + j // 4
                    act.wait_ge(s5gd.sem, s5gd.at(t, "q"))
                    act.activation(s5z[:, 0], s5z[:, 0], ACT.Tanh, scale=math.sqrt(2.0 / math.pi)).then_inc(s5ga.sem, 1)

            def s5_after(i, j):
                n = 8 * i + j + 1
                if not (isinstance(n, int) and n == S5_TILES):
                    s5_output_weights(n)

            s5_input_weights(0)
            s5_tables(0)
            s5_output_weights(0)
            product(by_name["in0"], take(lambda i, g: pr[:, bass.ds(HT + 2 * GT * i + GT * g, GT)]), s5_before, s5_after)
            act.wait_ge(tile_used, by_name["glu"]["u0"])
            for q in range(2):
                act.wait_ge(s5gd.sem, s5gd.at(4 * q + 3, "ys"))
                act.activation(ahi[:, 4 * q:4 * q + 4], pr[:, 4 * q:4 * q + 4], ACT.Copy).then_inc(s5_hi, 1)
            def glu(i, g, units):
                act.wait_ge(tile_used, units)
                act.activation(pg[:, g], pg[:, g], ACT.Tanh, scale=0.5).then_inc(glu_t, 1)
                act.wait_ge(glu_s, g + 1)
                act.activation(ahi[:, HT + GT * g:HT + GT * g + GT], pr[:, GT * g:GT * g + GT], ACT.Copy,
                               scale=0.5).then_inc(glu_hi, 1)
            product(by_name["glu"], glu)
            deltanet_act(act)
            product(by_name["out0"], take(lambda i, g: y[:, bass.ds(2 * GT * i + GT * g, GT)]))
            layer_norm(0)
            ffn(0)
            layer_norm(1)
            product(by_name["in1"], take(lambda i, g: pr1[:, bass.ds(2 * GT * i + GT * g, GT)]))
            attention_act(act)
            product(by_name["out1"], take(lambda i, g: y[:, bass.ds(2 * GT * i + GT * g, GT)]))
            layer_norm(2)
            ffn(1)
            layer_norm(3)

        @block.vector
        def _(dve):
            links = [0]

            def link(ins):
                links[0] += 1
                ins.then_inc(chain, 1)
                dve.wait_ge(chain, links[0])

            def ada_unit(ab, j, b):
                dve.wait_ge(ada_in[j % 2], 32 * ab + 16 * (j // 2 + 1))
                if j == 0:
                    dve.wait_ge(ada_summed, ab + (1 - b))
                for kk in range(UK):
                    k = UK * j + kk
                    if k == 0:
                        last = dve.tensor_scalar(acc[:, b], aw[:, 0, 0], cact[:, 0:1], None, ALU.mult)
                    else:
                        dve.wait_ge(ada_step, 16 * ab + (k + 5))
                        last = dve.scalar_tensor_tensor(acc[:, b], aw[:, j % 2, kk], cact[:, k:k + 1], acc[:, b],
                                                        ALU.mult, ALU.add)
                    last.then_inc(ada_step, 1)

            def ada_take(ab):
                dve.wait_ge(ada_summed, ab + 2)
                dve.tensor_tensor(mod[:, bass.ds(GT * ab, GT)], pm[:, 0:GT], adab[:, bass.ds(GT * ab, GT)],
                                  ALU.add).then_inc(mod_taken, 1)

            def split_lo(slot, half):
                dve.tensor_tensor(wlo[:, half], raw[:, slot], whi[:, half].bitcast(F32),
                                  ALU.subtract).then_inc(lo_done, 1)

            def product(p, evacuate, before=None, lag=0, skip_last=False):
                def body(i):
                    taken = 0
                    for j in range(p["bu"]):
                        for _ in range(ADA_AT[p["ada"]][j]):
                            ada_unit(p["ab0"] + taken // 4 + p["ada"] * i, taken % 4, taken // 4)
                            taken += 1
                        u = p["u0"] + p["bu"] * i + j
                        if before:
                            before(i, j)
                        if not (p["bodies"] == 1 and u + 2 >= n_units) and not (skip_last and j == p["bu"] - 1):
                            dve.wait_ge(hi_done, u + 3 - lag)
                            split_lo((j + 2 - lag) % 4, (j - lag) % 2)
                        if (j + 1) % p["units"] == 0 and evacuate:
                            evacuate(i, j // p["units"], u + 1)
                        if j in ADA_TAKE[p["ada"]]:
                            ada_take(p["ab0"] + ADA_TAKE[p["ada"]][j] + p["ada"] * i)
                        if lag and j % 4 == 3:
                            s5_gelu(2 * i + j // 4)
                bodies(dve, p["bodies"], body, peel=before is not None)

            def ffn(layer):
                for n, (first, groups) in enumerate(FFN_BLOCKS):
                    p = by_name[f"up{layer}{n}"]

                    def up(i, g, units, p=p, done=11 * layer + first):
                        dve.wait_ge(tile_used, units)
                        if g == 0:
                            dve.wait_ge(gate_t, done + i + 1)
                            dve.scalar_tensor_tensor(gs[:], gt[:], 1.0, pg[:, 0], ALU.add, ALU.mult).then_inc(grp_done, 1)
                        else:
                            dve.wait_ge(grp_done, p["g0"] + 2 * i + 3)
                            dve.scalar_tensor_tensor(gs[:], gs[:], 0.5, pg[:, 1], ALU.mult, ALU.mult).then_inc(grp_done, 1)
                            dve.wait_ge(hid_hi, done + i + 1)
                            dve.tensor_tensor(hlo[:, bass.ds(GT * i, GT)], gs[:],
                                              hhi[:, bass.ds(GT * i, GT)].bitcast(F32), ALU.subtract).then_inc(hid_lo, 1)
                    product(p, up)
                    p = by_name[f"down{layer}{n}"]

                    def down(i, g, units):
                        dst = y[:, bass.ds(2 * GT * i + GT * g, GT)]
                        dve.wait_ge(tile_used, units)
                        dve.tensor_tensor(dst, dst, pg[:, g % 2], ALU.add).then_inc(grp_done, 1)
                    product(p, down if n else None)

            def modulate(n, q):
                sh, sc = mod_cols(n)[:2]
                k = slice(4 * q, 4 * q + 4)
                link(dve.tensor_tensor(y[:, k], xT[:, k], along(onep[:, 0, k]), ALU.mult))
                dve.tensor_tensor(y[:, k], y[:, k], along(mod[:, sh + 4 * q:sh + 4 * q + 4]), ALU.add).then_inc(h_ready, 1)

            def modulate_lo(n, q):
                k = slice(4 * q, 4 * q + 4)
                dve.wait_ge(h_hi, 4 * n + q + 1)
                dve.tensor_tensor(alo[:, k], y[:, k], ahi[:, k].bitcast(F32), ALU.subtract).then_inc(act_ready, 1)

            def scale_ready(n):
                sh, sc, _, need, _ = mod_cols(n)
                dve.wait_ge(mod_taken, need + 1)
                link(dve.tensor_scalar(onep[:, 0], mod[:, sc:sc + KT], 1.0, None, ALU.add))

            def layer_norm(n, p):
                gate, need = mod_cols(n)[2], mod_cols(n)[4]
                dve.wait_ge(mod_taken, need + 1)
                link(dve.tensor_scalar(onep[:, 1], mod[:, gate:gate + KT], 1.0, None, ALU.add))
                dve.wait_ge(grp_done, p["g0"] + p["bodies"] * p["bg"] + 2)
                for q in range(4):
                    k = slice(4 * q, 4 * q + 4)
                    link(dve.tensor_tensor(y[:, k], y[:, k], along(onep[:, 1, k]), ALU.mult))
                    dve.scalar_tensor_tensor(xT[:, k], xT[:, k], ALPHA, y[:, k], ALU.mult, ALU.add).then_inc(ln_r, 1)
                dve.wait_ge(ln_mean, n + 1)
                for q in range(4):
                    k = slice(4 * q, 4 * q + 4)
                    dve.tensor_tensor(xT[:, k], xT[:, k], over(st[:, 0], 4), ALU.subtract).then_inc(ln_c, 1)
                if n < 3:
                    scale_ready(n + 1)
                dve.wait_ge(ln_std, n + 1)
                link(dve.reciprocal(st[:, 1], st[:, 1]))
                for q in range(4):
                    k = slice(4 * q, 4 * q + 4)
                    dve.tensor_tensor(xT[:, k], xT[:, k], over(st[:, 1], 4), ALU.mult).then_inc(ln_n, 1)
                for q in range(4 if n < 3 else 0):
                    dve.wait_ge(ln_gb, 4 * n + q + 1)
                    modulate(n + 1, q)
                    if q:
                        modulate_lo(n + 1, q - 1)
                if n < 3:
                    modulate_lo(n + 1, 3)

            for steps in (s5gd, dnd, scd, dad):
                dve.sem_inc(steps.sem, steps.start)
            dve.sem_inc(lo_done, 4)
            dve.sem_inc(grp_done, 2)
            dve.sem_inc(ada_step, 5)
            dve.sem_inc(mod_taken, 1)
            dve.memset(consts[:, 0:1], EPS)
            dve.memset(consts[:, 1:2], 1.5707962)
            dve.memset(consts[:, 3:4], 1e-6)
            dve.memset(consts[:, 4:5], 1.0).then_inc(vec_fix, 1)
            dve.wait_ge(vec_in, 16 * N_VEC_LOADS)
            dve.tensor_copy(vrow[64:96, 5].rearrange("p (g s) -> p g s", g=2),
                            vrow[64:96, 6, 0:2].unsqueeze(2).broadcast_to([32, 2, 64])).then_inc(vec_fix, 1)
            for n, (dst, bank, col, rows) in enumerate(VECS):
                dve.wait_ge(vec_turned, len(VECS))
                dve.tensor_copy(dst, bank[:, col:col + rows]).then_inc(vec_taken, 1)
            dve.wait_ge(c_tanh, 1)
            link(dve.scalar_tensor_tensor(cact[:], cact[:], 1.0, misc[:, 0:KT], ALU.add, ALU.mult))
            link(dve.tensor_scalar(cact[:], cact[:], 0.5, None, ALU.mult))

            are, aim = s5c[:, 0:32], s5c[:, 32:64]
            dve.wait_ge(s5_set.sem, s5_set.at(0, "delta"))
            dve.tensor_tensor(sv[:, 1], are, sv[:, 0], ALU.mult).then_inc(s5_setd.sem, 1)
            link(dve.scalar_tensor_tensor(sv[:, 3], aim, 1.0 / (2.0 * math.pi), sv[:, 0], ALU.mult, ALU.mult))
            link(dve.tensor_scalar(sv[:, 4], sv[:, 3], ROUND_1, ROUND_1, ALU.add, ALU.subtract))
            dve.tensor_tensor(sv[:, 4], sv[:, 3], sv[:, 4], ALU.subtract).then_inc(s5_setd.sem, 1)
            dve.wait_ge(s5_setd.sem, s5_setd.at(0, "f"))
            link(dve.tensor_copy(s5v[:, 0], sv[:, 4]))
            dve.wait_ge(s5_set.sem, s5_set.at(0, "sins"))
            link(dve.tensor_scalar(sv[:, 7], sv[:, 2], -1.0, 1.0, ALU.mult, ALU.add))
            link(dve.reciprocal(sv[:, 7], sv[:, 7]))
            link(dve.scalar_tensor_tensor(sv[:, 7], sv[:, 2], 2.0, sv[:, 7], ALU.mult, ALU.mult))
            link(dve.tensor_scalar(s5v[:, 2], sv[:, 7], 1.0, None, ALU.add))
            link(dve.scalar_tensor_tensor(sv[:, 8], sv[:, 6], -2.0, sv[:, 6], ALU.mult, ALU.mult))
            link(dve.scalar_tensor_tensor(sv[:, 9], sv[:, 8], 1.0, sv[:, 7], ALU.add, ALU.mult))
            link(dve.tensor_tensor(sv[:, 9], sv[:, 9], sv[:, 8], ALU.add))
            link(dve.tensor_tensor(sv[:, 10], s5v[:, 2], sv[:, 5], ALU.mult))
            link(dve.tensor_tensor(sv[:, 11], are, are, ALU.mult))
            link(dve.tensor_tensor(sv[:, 12], aim, aim, ALU.mult))
            link(dve.tensor_tensor(sv[:, 11], sv[:, 11], sv[:, 12], ALU.add))
            link(dve.reciprocal(sv[:, 11], sv[:, 11]))
            link(dve.tensor_tensor(sv[:, 12], sv[:, 9], are, ALU.mult))
            link(dve.tensor_tensor(sv[:, 13], sv[:, 10], aim, ALU.mult))
            link(dve.tensor_tensor(sv[:, 12], sv[:, 12], sv[:, 13], ALU.add))
            link(dve.tensor_tensor(sv[:, 12], sv[:, 12], sv[:, 11], ALU.mult))
            link(dve.tensor_tensor(sv[:, 13], sv[:, 10], are, ALU.mult))
            link(dve.tensor_tensor(sv[:, 14], sv[:, 9], aim, ALU.mult))
            link(dve.tensor_tensor(sv[:, 13], sv[:, 13], sv[:, 14], ALU.subtract))
            link(dve.tensor_tensor(sv[:, 13], sv[:, 13], sv[:, 11], ALU.mult))

            def ada_first(i):
                for b in range(2):
                    for j in range(4):
                        ada_unit(2 * i + b, j, b)
                for b in range(2):
                    ada_take(2 * i + b)
            for n in range(8):
                dve.wait_ge(x_turned, n + 1)
                dve.tensor_copy(xT[:, 2 * n:2 * n + 2], pgf[:, n % 4]).then_inc(x_taken, 1)
            bodies(dve, ADA_FIRST, ada_first)
            for j in (0, 1):
                dve.wait_ge(hi_done, j + 1)
                split_lo(j, j)
            scale_ready(0)
            for q in range(4):
                modulate(0, q)
                if q:
                    modulate_lo(0, q - 1)
            modulate_lo(0, 3)
            fre, fim = along(sv[:, 12], 16), along(sv[:, 13], 16)
            b1, b2 = s5z[:].rearrange("p a l -> p (a l)").rearrange("p (t c) -> p t c", c=16), \
                s5m2[:].rearrange("p a l -> p (a l)").rearrange("p (t c) -> p t c", c=16)
            dve.wait_ge(par_in, 16 * N_PAR_LOADS)
            link(dve.tensor_tensor(b1, s5br[:], fim, ALU.mult))
            link(dve.tensor_tensor(b2, s5bi[:], fim, ALU.mult))
            link(dve.tensor_tensor(s5br[:], s5br[:], fre, ALU.mult))
            link(dve.tensor_tensor(s5br[:], s5br[:], b2, ALU.subtract))
            link(dve.tensor_tensor(s5bi[:], s5bi[:], fre, ALU.mult))
            dve.tensor_tensor(s5bi[:], s5bi[:], b1, ALU.add).then_inc(s5_setd.sem, 1)
            dve.sem_inc(s5d.sem, s5d.n)
            dve.wait_ge(s5_setp.sem, 1)

            product(by_name["in0u"], None, skip_last=True)
            dve.wait_ge(ba_done, 1)
            dve.tensor_copy(ba[:], pb[:, 0:2 * N_SMALL].rearrange("p (c n) -> p c n", c=2)).then_inc(ba_taken, 1)
            def s5_chain(i, j):
                n = 8 * i + j
                r = n + 1
                bu = pb[:].rearrange("p (a l) -> p a l", a=2)
                dve.wait_ge(s5a.sem, s5a.at(r, "tab2"))
                dve.wait_ge(s5_bu, n + 2)
                dve.wait_ge(s5_y, n + 1)
                dve.tensor_tensor(s5m1[:], bu, over(s5tab[:, 1], 2), ALU.mult).then_inc(s5d.sem, 1)
                dve.tensor_tensor(s5m2[:, 0], bu[:, 1], s5tab[:, 0], ALU.mult).then_inc(s5d.sem, 1)
                dve.tensor_tensor(s5m2[:, 1], bu[:, 0], s5tab[:, 2], ALU.mult).then_inc(s5d.sem, 1)
                dve.wait_ge(s5d.sem, s5d.at(r, "m2b"))
                dve.tensor_tensor(s5z[:], s5m1[:], s5m2[:], ALU.add).then_inc(s5d.sem, 1)
                dve.wait_ge(s5d.sem, s5d.at(r, "z"))
                decay = s5v[:, 2, bass.ds(n, 1)].broadcast_to([P, L])
                dve.tensor_tensor_scan(s5m1[:, 0], decay, s5z[:, 0], 0.0, ALU.mult, ALU.add).then_inc(s5d.sem, 1)
                dve.tensor_tensor_scan(s5m1[:, 1], decay, s5z[:, 1], 0.0, ALU.mult, ALU.add).then_inc(s5d.sem, 1)
                dve.wait_ge(s5d.sem, s5d.at(r, "si"))
                dve.tensor_tensor(s5m2[:], s5m1[:], s5tab[:, 1:3], ALU.mult).then_inc(s5d.sem, 1)
                dve.tensor_tensor(s5z[:], s5m1[:], s5tab[:, 0:2], ALU.mult).then_inc(s5d.sem, 1)

            def s5_gelu(t):
                def step(name, ins):
                    ins.then_inc(s5gd.sem, 1)
                    dve.wait_ge(s5gd.sem, s5gd.at(t, name))

                dve.wait_ge(s5_y, 4 * t + 5)
                step("yv", dve.scalar_tensor_tensor(s5z[:, 1:2], pr[:, bass.ds(t, 1)], misc[:, bass.ds(40 + t, 1)],
                                                    pc[:, 0:L].unsqueeze(1), ALU.mult, ALU.add))
                step("y2", dve.tensor_tensor(s5z[:, 0], s5z[:, 1], s5z[:, 1], ALU.mult))
                step("p", dve.tensor_scalar(s5z[:, 0], s5z[:, 0], 0.044715, 1.0, ALU.mult, ALU.add))
                dve.tensor_tensor(s5z[:, 0], s5z[:, 0], s5z[:, 1], ALU.mult).then_inc(s5gd.sem, 1)
                dve.wait_ge(s5ga.sem, s5ga.at(t, "th"))
                step("s", dve.scalar_tensor_tensor(s5z[:, 0], s5z[:, 0], 1.0, s5z[:, 1], ALU.add, ALU.mult))
                dve.tensor_scalar(pr[:, bass.ds(t, 1)], s5z[:, 0:1], 0.5, None, ALU.mult).then_inc(s5gd.sem, 1)

            product(by_name["in0"], None, s5_chain, lag=1)
            for q in range(2):
                dve.wait_ge(s5_hi, q + 1)
                dve.tensor_tensor(alo[:, 4 * q:4 * q + 4], pr[:, 4 * q:4 * q + 4],
                                  ahi[:, 4 * q:4 * q + 4].bitcast(F32), ALU.subtract).then_inc(s5_lo, 1)
            dve.wait_ge(hi_done, by_name["glu"]["u0"] + 2)
            split_lo(1, 1)

            def glu(i, g, units):
                k = slice(GT * g, GT * g + GT)
                dve.wait_ge(glu_t, g + 1)
                dve.scalar_tensor_tensor(pr[:, k], pg[:, g], 1.0, pr[:, k], ALU.add, ALU.mult).then_inc(glu_s, 1)
                dve.wait_ge(glu_hi, g + 1)
                k2 = slice(HT + GT * g, HT + GT * g + GT)
                dve.scalar_tensor_tensor(alo[:, k2], pr[:, k], 0.5, ahi[:, k2].bitcast(F32), ALU.mult,
                                         ALU.subtract).then_inc(grp_done, 1)
            product(by_name["glu"], glu)
            deltanet_dve(dve, link, ada_unit, ada_take)
            product(by_name["out0"], None)
            layer_norm(0, by_name["out0"])
            ffn(0)
            layer_norm(1, by_name["down02"])
            product(by_name["in1"], None)
            attention_dve(dve)
            product(by_name["out1"], None)
            layer_norm(2, by_name["out1"])
            ffn(1)
            layer_norm(3, by_name["down12"])
            for n in range(8):
                dve.wait_ge(o_turned, n + 1)
                dve.tensor_copy(orow[:, n // 4, GROUP * (n % 4):GROUP * (n % 4 + 1)], pgf[:, n % 4]).then_inc(o_taken, 1)

        @block.tensor
        def _(pe):
            def ada_sum(ab, b):
                pe.wait_ge(ada_step, 16 * ab + 21)
                pe.wait_ge(mod_taken, ab + 1)
                for t in range(GT):
                    last = pe.matmul(pm[:, t:t + 1], acc[:, b, P * t:P * t + P], ones[:, 0:1], start=True, stop=True)
                last.then_inc(ada_summed, 1)

            def product(p, ready, hi=None, lo=None, mid=None, after=None):
                hi, lo = hi if hi is not None else ahi, lo if lo is not None else alo

                def body(i):
                    for j in range(p["bu"]):
                        u = p["u0"] + p["bu"] * i + j
                        g, q = j // p["units"], j % p["units"]
                        pe.wait_ge(lo_done, u + 5)
                        ready(q)
                        if q == 0:
                            pe.wait_ge(grp_done, p["g0"] + p["bg"] * i + g + 1)
                        for kk in range(UK):
                            k = UK * q + kk
                            if mid and kk == UK // 2:
                                mid(i, j)
                            for n in range(GT):
                                dst, cols = pg[:, g % 2, n], slice(P * n, P * n + P)
                                pe.matmul(dst, whi[:, j % 2, kk, cols], hi[:, k], start=(k == 0 and n % 2 == 0),
                                          stop=False, skip_group_check=True)
                                pe.matmul(dst, whi[:, j % 2, kk, cols], lo[:, k], start=False,
                                          stop=False, skip_group_check=True)
                                last = pe.matmul(dst, wlo[:, j % 2, kk, cols], hi[:, k], start=False,
                                                 stop=(k == UK * p["units"] - 1), skip_group_check=True)
                        last.then_inc(tile_used, 1)
                        if j in ADA_SUM[p["ada"]]:
                            b = ADA_SUM[p["ada"]][j]
                            ada_sum(p["ab0"] + b + p["ada"] * i, b)
                        if after:
                            after(i, j)
                bodies(pe, p["bodies"], body, peel=after is not None)

            def on_act(n):
                return lambda q: pe.wait_ge(act_ready, 4 * n + q + 1)

            def ffn(layer):
                for n, (first, groups) in enumerate(FFN_BLOCKS):
                    product(by_name[f"up{layer}{n}"], on_act(2 * layer + 1))
                    product(by_name[f"down{layer}{n}"],
                            lambda q, done=11 * layer + first + groups: pe.wait_ge(hid_lo, done), hhi, hlo)

            def layer_norm(n):
                for k in range(KT):
                    if k % 4 == 0:
                        pe.wait_ge(ln_r, 4 * n + k // 4 + 1)
                    last = pe.matmul(pa[:, 0:L], ones[:], xT[:, k], start=(k == 0), stop=(k == KT - 1))
                last.then_inc(ln_sum, 1)
                for k in range(KT):
                    if k % 4 == 0:
                        pe.wait_ge(ln_sq, 4 * n + k // 4 + 1)
                    last = pe.matmul(pb[:, 0:L], ones[:], y[:, k], start=(k == 0), stop=(k == KT - 1))
                last.then_inc(ln_var, 1)

            pe.sem_inc(ada_summed, 1)
            for steps in (dne, dae_):
                pe.sem_inc(steps.sem, steps.start)
            pe.wait_ge(const_done, 1)
            pe.wait_ge(vec_in, 16 * N_VEC_LOADS)
            pe.wait_ge(vec_fix, 2)
            for n, (_, bank, col, rows) in enumerate(VECS):
                pe.transpose(bank[:, col:col + rows], vrow[0:rows, n], ident[0:rows, 0:rows]).then_inc(vec_turned, 1)
            pe.wait_ge(x_in, 16)
            for n in range(8):
                if n >= 4:
                    pe.wait_ge(x_taken, n - 3)
                for t in range(2):
                    for b in range(2):
                        f = 2 * n + t
                        last = pe.transpose(pgf[:, n % 4, L * t + P * b:L * t + P * b + P], xrow[:, b, P * f:P * f + P],
                                            ident[:])
                last.then_inc(x_turned, 1)

            def ada_first(i):
                for b in range(2):
                    ada_sum(2 * i + b, b)
            bodies(pe, ADA_FIRST, ada_first)
            pe.wait_ge(x_taken, 8)
            product(by_name["in0u"], on_act(0))
            pe.wait_ge(par_in, 16 * N_PAR_LOADS)
            for b in range(2):
                for k in range(KT):
                    for n, half in enumerate((ahi, alo)):
                        last = pe.matmul(pb[:, N_SMALL * b:N_SMALL * b + N_SMALL], half[:, k, P * b:P * b + P].bitcast(F32),
                                         wba[:, k], start=(k == 0 and n == 0), stop=(k == KT - 1 and n == 1))
            last.then_inc(ba_done, 1)
            pe.wait_ge(ba_taken, 1)
            pe.wait_ge(grp_done, by_name["in0"]["g0"] + 2)
            for steps in (s5_turned, s5_bu, s5_y):
                pe.sem_inc(steps, 1)

            def s5_turn(n):
                pe.wait_ge(s5p.sem, s5p.at(n + 1, "pad"))
                pe.wait_ge(s5a.sem, s5a.at(n, "wneg"))
                for m in range(4):
                    last = pe.transpose(pa[:, P * m:P * m + P], s5pad[:, m], ident[:])
                last.then_inc(s5_turned, 1)

            def s5_in(n, t):
                pe.wait_ge(s5a.sem, s5a.at(n + 1, "wb"))
                pe.wait_ge(s5d.sem, s5d.at(n, "m2b"))
                for m in range(2):
                    last = pe.matmul(pb[:, L * m:L * m + L], s5w[:, m], pr[:, bass.ds(t, 1)], start=True, stop=True)
                last.then_inc(s5_bu, 1)

            def s5_out(n, t, s):
                if s == 0:
                    pe.wait_ge(s5gd.sem, s5gd.begin(t))
                pe.wait_ge(s5d.sem, s5d.at(n + 1, "p2"))
                pe.wait_ge(s5a.sem, s5a.at(n + 1, "wneg"))
                for m, (w, z) in enumerate(((2, s5m2), (3, s5z))):
                    for h in range(2):
                        last = pe.matmul(pc[:, 0:L], s5w[:, w], z[:, h], start=(s == 0 and m == 0 and h == 0),
                                         stop=(s == 3 and m == 1 and h == 1))
                last.then_inc(s5_y, 1)

            def s5_mid(i, j):
                n = 8 * i + j + 1
                if not (isinstance(n, int) and n == S5_TILES):
                    s5_turn(n)

            def s5_after(i, j):
                n = 8 * i + j
                s5_out(n, 2 * i + j // 4, j % 4)
                if not (isinstance(n, int) and n == S5_TILES - 1):
                    s5_in(n + 1, 2 * i + (j + 1) // 4)

            s5_turn(0)
            s5_in(0, 0)
            product(by_name["in0"], on_act(0), mid=s5_mid, after=s5_after)
            product(by_name["glu"], lambda q: pe.wait_ge(s5_lo, q + 1))
            deltanet_pe(pe, ada_sum)
            product(by_name["out0"], lambda q: pe.wait_ge(dnd.sem, dnd.at(3, "lo")))
            layer_norm(0)
            ffn(0)
            layer_norm(1)
            product(by_name["in1"], on_act(2))
            attention_pe(pe)
            product(by_name["out1"], lambda q: (pe.wait_ge(scd.sem, scd.at(HT - 1, "lo")),
                                                pe.wait_ge(dad.sem, dad.at(DA_HEADS - 1, "lo"))))
            layer_norm(2)
            ffn(1)
            layer_norm(3)
            for n in range(8):
                b, q = n // 4, n % 4
                pe.wait_ge(ln_gb, 4 * 3 + q + 1)
                if n >= 4:
                    pe.wait_ge(o_taken, n - 3)
                for t in range(4):
                    last = pe.transpose(pgf[:, n % 4, P * t:P * t + P], xT[:, 4 * q + t, P * b:P * b + P], ident[:])
                last.then_inc(o_turned, 1)

        @block.gpsimd
        def _(pool):
            pool.sem_inc(dnp.sem, dnp.start)
            pool.memset(pidle[:], 0.0)
            pool.memset(ones[:], 1.0)
            pool.memset(ident[:], 0.0).then_inc(pool_c, 1)
            pool.wait_ge(pool_c, 1)
            pool.affine_select(out=ident[:], in_=ident[:], compare_op=ALU.not_equal, fill=1.0, base=0,
                               pattern=[[-1, P]], channel_multiplier=1).then_inc(const_done, 1)
            for s in range(4):
                pool.memset(s5mk[:, s], 1.0)
                pool.memset(s5mt[:, s], 1.0)
            pool.iota(tcol[:], [[1, L]], base=-L // 2, channel_multiplier=0, allow_small_or_imprecise_dtypes=True).then_inc(pool_c, 1)
            pool.wait_ge(pool_c, 2)
            for s in range(4):
                for h in range(2):
                    g = 2 * s + h
                    v = s5mk[:, s, 64 * h:64 * h + 64]
                    link_pool(pool, pool.affine_select(out=v, in_=v, compare_op=ALU.is_ge, fill=0.0, base=-16 * g,
                                                       pattern=[[0, 64]], channel_multiplier=1))
                    link_pool(pool, pool.affine_select(out=v, in_=v, compare_op=ALU.is_ge, fill=0.0, base=16 * g + 15,
                                                       pattern=[[0, 64]], channel_multiplier=-1))
                v = s5mt[:, s]
                for h in range(8):
                    w = v[:, 16 * h:16 * h + 16]
                    if h == 2 * s:
                        ok = dict(compare_op=ALU.is_ge, base=63, channel_multiplier=-1)
                    elif h == 2 * s + 1:
                        ok = dict(compare_op=ALU.is_ge, base=-64, channel_multiplier=1)
                    else:
                        ok = dict(compare_op=ALU.is_ge, base=-1, channel_multiplier=0)
                    link_pool(pool, pool.affine_select(out=w, in_=w, fill=0.0, pattern=[[0, 16]], **ok))
            pool.sem_inc(s5_setp.sem, 1)
            pool.wait_ge(s5_setd.sem, s5_setd.at(0, "done"))
            pool.sem_inc(s5p.sem, s5p.n)
            with pool.Fori(0, HT) as t:
                for s in range(4):
                    i = 4 * t + s + 1
                    k = 4 * t + s
                    a0, a1 = s5arg[:, 0], s5arg[:, 1]
                    pool.wait_ge(s5a.sem, s5a.at(i - 1, "tab2"))
                    pool.tensor_tensor(a0, tcol[:], s5v[:, 0, bass.ds(k, 1)].broadcast_to([P, L]), ALU.mult).then_inc(s5p.sem, 1)
                    pool.wait_ge(s5p.sem, s5p.at(i, "turns"))
                    carry(pool)
                    pool.tensor_scalar(a1, a0, ROUND_1, ROUND_1, ALU.add, ALU.subtract).then_inc(s5p.sem, 1)
                    pool.wait_ge(s5p.sem, s5p.at(i, "whole"))
                    pool.tensor_tensor(a0, a0, a1, ALU.subtract).then_inc(s5p.sem, 1)
                    pool.wait_ge(s5p.sem, s5p.at(i, "sine"))
                    carry(pool)
                    pool.tensor_scalar(a1, a0, 0.25, -1.0, ALU.is_gt, ALU.mult).then_inc(s5p.sem, 1)
                    pool.wait_ge(s5p.sem, s5p.at(i, "over"))
                    pool.tensor_tensor(a1, a0, a1, ALU.add).then_inc(s5p.sem, 1)
                    pool.wait_ge(s5_turned, i)
                    for n, src in enumerate((s5br, s5bi)):
                        pool.tensor_tensor(s5pad[:, n].rearrange("p (h c) -> p h c", c=16),
                                           src[:, bass.ds(4 * t + s, 1)].broadcast_to([P, 8, 16]),
                                           s5mt[:, s].rearrange("p (h c) -> p h c", c=16), ALU.mult)
                    for n, src in enumerate((s5cr, s5ci)):
                        last = pool.tensor_tensor(s5pad[:, 2 + n].rearrange("p (h c) -> p h c", c=64),
                                                  src[:, bass.ds(t, 1)].broadcast_to([P, 2, 64]),
                                                  s5mk[:, s].rearrange("p (h c) -> p h c", c=64), ALU.mult)
                    last.then_inc(s5p.sem, 1)
            deltanet_pool(pool)
            attention_pool(pool)


_INS = ['x', 'c', 'ada_w', 'ada_b', 'ln1_g', 'ln1_b', 'ln2_g', 'ln2_b', 'ffn_w_gate', 'ffn_w_up', 'ffn_w_down',
        'ab_w_in', 'ab_w_out', 'dn_conv_w', 'dn_a_log', 'dn_dt_bias', 'dn_norm_g',
        's5_a_re', 's5_a_im', 's5_b_re', 's5_b_im', 's5_c_re', 's5_c_im', 's5_d', 's5_log_dt', 's5_w_glu',
        'cd_w_in', 'cd_w_out', 'sc_conv_w', 'da_lq1', 'da_lk1', 'da_lq2', 'da_lk2', 'da_norm_g']
_OUTS = [((1, 256, 2048), 'float32')]


def kernel(**inputs):
    import numpy as _np
    import concourse.bacc as _bacc
    from concourse import mybir as _mybir
    from concourse.bass_utils import run_bass_kernel_spmd as _run

    nc = _bacc.Bacc("TRN2", target_bir_lowering=False, num_devices=1)
    arrays, args = {}, []
    for name in _INS:
        a = _np.ascontiguousarray(inputs[name])
        arrays[f"in_{name}_dram"] = a
        args.append(nc.dram_tensor(f"in_{name}_dram", a.shape, _mybir.dt.from_np(a.dtype), kind="ExternalInput").ap())
    for i, (shape, dtype) in enumerate(_OUTS):
        dt = _mybir.dt.from_np(_np.dtype(dtype))
        args.append(nc.dram_tensor(f"out_{i}_dram", shape, dt, kind="ExternalOutput").ap())
    build(nc, *args)
    r = _run(nc, [arrays], core_ids=[0])
    got = tuple(r.results[0][f"out_{i}_dram"] for i in range(len(_OUTS)))
    return got[0]
```

```python
import math
from contextlib import ExitStack

import concourse.bass as bass
from concourse import mybir

F32 = mybir.dt.float32
F32R = mybir.dt.float32r
ALU = mybir.AluOpType
ACT = mybir.ActivationFunctionType
AX_X = mybir.AxisListType.X

P = 128
D = 2048
L = 256
DEPTH = 2
KT = D // P
D_FF = ((8 * D // 3 + 255) // 256) * 256
FFN_GROUPS = D_FF // 512
HALF = D // 2
HT = HALF // P
ALPHA = (2.0 * DEPTH) ** 0.25
EPS = 1e-5
LAMBDA_INIT = 0.8 - 0.6 * math.exp(-0.3)
DA_HEADS = HALF // (2 * P)
S5_TILES = 64 * 64 // P
GROUP = 512
GT = GROUP // P
UK = 4
ROUND_1 = 1.5 * 2.0 ** 23
BIG = -1.0e30
N_ADA = 6 * KT
FFN_BLOCKS = [(0, 4), (4, 4), (8, 3)]
AB_SMALL = 4 * HALF
N_SMALL = 2 * HT
LAYER_BLOCKS = 6 * D // GROUP
LEVELS = 7

ADA_FIRST = 4
FIRST_SLOTS = 8
ADA_FREE = 4 * (FIRST_SLOTS - 1) + 1
TWO_PI_LOW = 6.283185
N_VEC_LOADS, N_PAR_LOADS = 19, 7

ADA_AT = {(0, 4): [0] * 4, (0, 8): [0] * 8, (0, 12): [0] * 12, (1, 8): [0, 1, 1, 0, 0, 1, 1, 0],
          (1, 12): [0, 1, 0, 0, 1, 0, 0, 1, 0, 0, 1, 0], (2, 8): [1, 1, 1, 1, 1, 1, 2, 0]}
ADA_SUM = {0: {}, 2: {4: 0, 7: 1}}
ADA_TAKE = {0: {}, 2: {5: 0, 7: 1}}


class Steps:

    def __init__(self, semaphore, names, start=0):
        self.sem, self.names, self.n, self.start = semaphore, names.split(), len(names.split()), start

    def at(self, i, name):
        return i * self.n + (self.names.index(name) + 1 + self.start)

    def begin(self, i):
        return i * self.n + self.start


def plan(w):
    products = []

    def add(name, bodies, groups, units, k0=0, ada=0):
        products.append(dict(name=name, bodies=bodies, groups=groups, units=units, k0=k0, ada=ada))

    def ffn(layer, ada_up, ada_down):
        g, u, d = w["gate"][layer], w["up"][layer], w["down"][layer]
        for n, (first, groups) in enumerate(FFN_BLOCKS):
            add(f"up{layer}{n}", groups, [(g, first * GROUP, GROUP), (u, first * GROUP, GROUP)], 4, ada=ada_up[n])
            if groups == 4:
                add(f"down{layer}{n}", 2, [(d, 0, 2 * GROUP), (d, GROUP, 2 * GROUP)], 4, k0=first * GT, ada=ada_down)
            else:
                add(f"down{layer}{n}", 1, [(d, j * GROUP, 0) for j in range(4)], groups, k0=first * GT, ada=ada_down)

    pair = [(0, 2), (1, 2)]
    u_col = AB_SMALL + N_SMALL
    add("in0u", 1, [(w["in0"], u_col + GROUP * a, 0) for a, _ in pair], 4, ada=2)
    add("in0", 4, [(w["in0"], GROUP * a, 2 * GROUP) for a, _ in pair], 4, ada=0)
    add("glu", 1, [(w["glu"], GROUP * a, 0) for a, _ in pair], 2)
    products[-1]["ada_after"] = 2 * HT // 2
    add("out0", 2, [(w["out0"], GROUP * a, 2 * GROUP) for a, _ in pair], 4, ada=1)
    ffn(0, (1, 1, 1), 1)
    add("in1", 6, [(w["in1"], GROUP * a, 2 * GROUP) for a, _ in pair], 4, ada=1)
    add("out1", 2, [(w["out1"], GROUP * a, 2 * GROUP) for a, _ in pair], 4, ada=1)
    ffn(1, (1, 0, 0), 0)
    u = g = 0
    ab = 2 * ADA_FIRST
    for p in products:
        last = {p["units"] * len(p["groups"]) - 1: 0}
        p.update(sums=ADA_SUM[p["ada"]] if p["ada"] != 1 else last, takes=ADA_TAKE[p["ada"]] if p["ada"] != 1 else last)
        p.update(u0=u, g0=g, ab0=ab, bu=p["units"] * len(p["groups"]), bg=len(p["groups"]))
        u += p["bodies"] * p["bu"]
        g += p["bodies"] * p["bg"]
        ab += p["bodies"] * p["ada"]
        p["ab1"] = ab
        ab += p.get("ada_after", 0)
        assert u % 4 == 0 and g % 2 == 0
    assert ab == 2 * N_ADA // GT, ab
    return products, u


def build(nc, x, c, ada_w, ada_b, ln1_g, ln1_b, ln2_g, ln2_b, ffn_w_gate, ffn_w_up, ffn_w_down,
          ab_w_in, ab_w_out, dn_conv_w, dn_a_log, dn_dt_bias, dn_norm_g,
          s5_a_re, s5_a_im, s5_b_re, s5_b_im, s5_c_re, s5_c_im, s5_d, s5_log_dt, s5_w_glu,
          cd_w_in, cd_w_out, sc_conv_w, da_lq1, da_lk1, da_lq2, da_lk2, da_norm_g, out):
    products, n_units = plan(dict(
        gate=[ffn_w_gate[i] for i in range(DEPTH)], up=[ffn_w_up[i] for i in range(DEPTH)],
        down=[ffn_w_down[i] for i in range(DEPTH)], in0=ab_w_in[0], glu=s5_w_glu[0], out0=ab_w_out[0],
        in1=cd_w_in[0], out1=cd_w_out[0]))
    by_name = {p["name"]: p for p in products}

    ctx = ExitStack()
    with ctx:
        def sb(name, shape, dt=F32):
            return ctx.enter_context(nc.sbuf_tensor(name, shape, dt))

        def sem(name):
            return ctx.enter_context(nc.semaphore(name))

        def shared(layout):
            with ExitStack() as s:
                return [s.enter_context(nc.sbuf_tensor(n, shape, F32 if not dt else dt[0])) for n, shape, *dt in layout]

        raw = sb("w_raw", [P, 4, UK, GROUP])
        whi = sb("w_hi", [P, 2, UK, GROUP], F32R)
        aw = sb("ada_units", [P, 2, UK, GROUP])
        acc = sb("ada_acc", [P, 2, GROUP])
        xT = sb("xT", [P, KT, L])
        (first6,) = shared([("ada_first", [P, FIRST_SLOTS - 2, UK, GROUP])])
        wlo = sb("w_lo", [P, 2, UK, GROUP], F32R)
        ahi = sb("act_hi", [P, KT, L], F32R)
        alo = sb("act_lo", [P, KT, L], F32R)
        mod = sb("mod", [P, DEPTH * N_ADA])
        adab = sb("ada_b_cols", [P, DEPTH * N_ADA])
        lnc = sb("ln_cols", [P, 4 * DEPTH * KT])
        dcw = sb("dn_conv_cols", [P, 4 * 3 * HT])
        misc = sb("misc_cols", [P, 64])
        ident = sb("ident", [P, P])
        ones = sb("ones", [P, P])
        cact = sb("c_act", [P, KT])
        onep = sb("one_plus", [P, 2, KT])
        fold = sb("ln_fold", [P, 4, KT])
        pidle = sb("pool_idle", [P, 2])
        consts = sb("consts", [P, 8])
        s5c = sb("s5_cols", [P, 3 * S5_TILES])
        wba = sb("w_small", [P, KT, N_SMALL])
        ba = sb("ba", [P, 2, N_SMALL])
        dnb = sb("dn_small", [P, 2, HT])

        y, hhi, hlo, gt, gs, st = shared([("y", [P, KT, L]), ("hid_hi", [P, 16, L], F32R), ("hid_lo", [P, 16, L], F32R),
                                      ("gate_t", [P, GT, L]), ("gate_s", [P, GT, L]),
                                          ("ln_stat", [P, 2, L])])
        xrow, vrow = shared([("x_rows", [P, 2, D]), ("vec_rows", [P, 7, P])])
        (orow,) = shared([("out_rows", [P, 2, D])])
        (pr, s5br, s5bi, s5cr, s5ci, s5mk, s5mt, s5pad, s5w, s5tab, s5arg, s5m1, s5m2, s5z, s5v, tcol, s5g) = shared([
            ("proj0", [P, 5 * HT, L]),
            ("s5_b_re_t", [P, S5_TILES, 16]), ("s5_b_im_t", [P, S5_TILES, 16]),
            ("s5_c_re_t", [P, HT, 64]), ("s5_c_im_t", [P, HT, 64]),
            ("s5_mask", [P, 4, P]), ("s5_mask_t", [P, 4, P]),
            ("s5_pad", [P, 4, P]), ("s5_w", [P, 4, P]), ("s5_tab", [P, 3, L]), ("s5_arg", [P, 2, L]),
            ("s5_m1", [P, 2, L]), ("s5_m2", [P, 2, L]), ("s5_z", [P, 2, L]),
            ("s5_vec", [P, 3, S5_TILES]), ("s5_time", [P, L]), ("s5_gelu", [P, 1, L])])
        (pp, at, vn, sst, kt, _, lm, tri, dng, cv, sq, m, mb, d, dt, vt, rr, cq) = shared([
            ("dn_p", [P, 4, P]), ("dn_at", [P, 4, P]), ("dn_vnew", [P, 4, P]), ("dn_state", [P, 2, P]),
            ("dn_ktok", [P, 2, P]), ("dn_proj0", [P, 4 * HT, L]), ("dn_levels", [P, LEVELS, P]),
            ("dn_tri", [P, P]), ("dn_gates", [P, 10, 2, HT]), ("dn_conv", [P, 6, L]), ("dn_sq", [P, 2, L]),
            ("dn_m", [P, 4, P]), ("dn_mb", [P, 4, P]), ("dn_d", [P, 4, P]), ("dn_dt", [P, 4, P]),
            ("dn_vtok", [P, 4, P]), ("dn_r", [P, 4, P]),
            ("dn_conv_q", [P, 2, L])])
        (pr1, scm, scv, daq, dand, das, dae, dac, dact, davt, dao, dav) = shared([
            ("proj1", [P, 6 * HT, L]), ("sc_m", [P, 2, L]), ("sc_conv", [P, 2, L]), ("da_q", [P, 2, L]),
            ("da_nd", [P, 3 * P]), ("da_s", [P, 2, L]), ("da_e", [P, 2, L]),
            ("da_c", [P, L]), ("da_ct", [P, 3, P]), ("da_vtok", [P, 2, L]), ("da_o", [P, 2, L]),
            ("da_vec", [P, 48])])
        first_slots = [aw[:, n] for n in range(2)] + [first6[:, n] for n in range(FIRST_SLOTS - 2)]
        pg = ctx.enter_context(nc.psum_tensor("groups", [P, 2, GT, L], F32))
        pgf = pg[:].rearrange("p a (b c) t -> p (a b) (c t)", b=2)
        pm, pa, pb, pc = [ctx.enter_context(nc.psum_tensor(n, [P, 512], F32)) for n in ("pm", "pa", "pb", "pc")]

        raw_in = [sem(f"raw_in{i}") for i in range(4)]
        ada_in = [sem(f"ada_in{i}") for i in range(2)]
        ada_in_first = [sem(f"ada_in_first{i}") for i in range(FIRST_SLOTS)]
        ada_in_pool = [sem(f"ada_in_pool{i}") for i in range(2)]
        hi_done, lo_done = sem("hi_done"), sem("lo_done")
        tile_used = sem("tile_used")
        grp_done = sem("grp_done")
        gate_t, hid_hi, hid_lo = sem("gate_t"), sem("hid_hi"), sem("hid_lo")
        ada_step = sem("ada_step")
        ada_summed, mod_taken = sem("ada_summed"), sem("mod_taken")
        vec_in, x_in, par_in, vec_fix = sem("vec_in"), sem("x_in"), sem("par_in"), sem("vec_fix")
        const_done, vec_turned, vec_taken = sem("const_done"), sem("vec_turned"), sem("vec_taken")
        x_turned, x_taken, c_tanh, c_done = sem("x_turned"), sem("x_taken"), sem("c_tanh"), sem("c_done")
        h_ready, h_hi, act_ready, folded = sem("h_ready"), sem("h_hi"), sem("act_ready"), sem("folded")
        glu_t, glu_s, glu_hi = sem("glu_t"), sem("glu_s"), sem("glu_hi")
        chain, pool_chain, pool_c = sem("dve_chain"), sem("pool_chain"), sem("pool_const")
        pool_links = [0]
        ln_sum, ln_mean, ln_c, ln_sq = sem("ln_sum"), sem("ln_mean"), sem("ln_c"), sem("ln_sq")
        ln_var, ln_std, ln_n, ln_gb = sem("ln_var"), sem("ln_std"), sem("ln_n"), sem("ln_gb")
        o_turned, o_taken, out_done = sem("o_turned"), sem("o_taken"), sem("out_done")

        s5_set = Steps(sem("s5_set_act"), "delta tanh sins")
        s5_setd = Steps(sem("s5_set_dve"), "x f done")
        s5_setp = Steps(sem("s5_set_pool"), "masks")
        s5p = Steps(sem("s5_pool"), "pad turns whole sine over cosine")
        s5_turned, s5_bu, s5_y = sem("s5_turned"), sem("s5_bu"), sem("s5_y")
        s5a = Steps(sem("s5_act"), "wb tab0 tab1 tab2 wc wneg")
        s5d = Steps(sem("s5_dve"), "m1 m2a m2b z sr si p1 p2 q1 q2")
        s5ga = Steps(sem("s5_gelu_act"), "th")
        s5_read = sem("s5_read")
        s5_hi, s5_lo = sem("s5_hi"), sem("s5_lo")
        s5gd = Steps(sem("s5_gelu_dve"), "y2 p q s ys", start=1)
        ba_done, ba_taken = sem("ba_done"), sem("ba_taken")

        dna_set = Steps(sem("dn_set_act"), "tanh ealog eabs ln eG tail0")
        dnd_set = Steps(sem("dn_set_dve"), "pre g arg done")
        dne_set = Steps(sem("dn_set_pe"), "cum")
        dnp_set = Steps(sem("dn_set_pool"), "tri masks")
        dnd = Steps(sem("dn_dve"), "gt bt sl0 sl1 sl2 nq nk dm m0 m1 am r0 "
                    + " ".join(f"d{k} dt{k}" for k in range(LEVELS - 1)) + f" dt{LEVELS - 1}"
                    + " r1a r1 o1 rmsr on zs yz lo", start=1)
        dnc = Steps(sem("dn_conv"), " ".join(f"c{mm}{tap}" for mm in range(3) for tap in range(4)), start=1)
        dna = Steps(sem("dn_act"), "th0 th1 th2 sqq sqk lnq lnk stq stk zt ed vt kt "
                    + " ".join(f"p{k}" for k in range(LEVELS)) + f" vn0 S vn1 oc ss rs hi", start=1)
        dne = Steps(sem("dn_pe"), "gi nq nk gram bi vt kt "
                    + " ".join(f"p{k} y{k} x{k}" for k in range(LEVELS - 1))
                    + " p{0} x{0} vn0 S kS vn1 ov qS turn".format(LEVELS - 1), start=1)
        dnp = Steps(sem("dn_pool"), "init " + " ".join(f"mb{k}" for k in range(LEVELS)) + " at", start=1)

        scd = Steps(sem("sc_dve"), "m c0 c1 c2 g", start=1)
        sc_hi, sc_lo = sem("sc_hi"), sem("sc_lo")
        da_setp, da_setd = Steps(sem("da_set_pool"), "nd"), Steps(sem("da_set_dve"), "prod lam")
        da_sete, da_seta = Steps(sem("da_set_pe"), "sum"), Steps(sem("da_set_act"), "exp")
        dad = Steps(sem("da_dve"), "q v s0 mx0 ng0 r0 rl0 t0 c0 s1 mx1 ng1 r1 rl1 t1 c1 rr on og hi lo", start=1)
        daa = Steps(sem("da_act"), "vt e0 ct0 e1 ct1 o sq std", start=1)
        dae_ = Steps(sem("da_pe"), "sc0 sc1 vt ct0 pv0 ct1 pv1 ss", start=1)

        VECS = [(adab[:, 0:96], pa, 0, 96), (adab[:, 96:192], pa, 96, 96), (lnc[:], pa, 192, 128), (dcw[:], pa, 320, 96),
                (misc[:, 0:55], pb, 0, 55), (s5c[:], pb, 128, 96)]
        sv = s5m1[:].rearrange("p a l -> p (a l)").rearrange("p (k t) -> p k t", t=S5_TILES)

        def along(cols, n=L):
            return cols.unsqueeze(2).broadcast_to([cols.shape[0], cols.shape[1], n])

        def over(rows, k):
            return rows.unsqueeze(1).broadcast_to([rows.shape[0], k, rows.shape[1]])

        BETA, GDEC, GCUM, EG, BEG, TAIL, EALOG, XA, SUMSQ, EABS = range(10)
        glu_end = by_name["glu"]["g0"] + 4
        pair_v = lambda buf: buf[:].rearrange("p (a c) l -> p a (c l)", c=2)
        prob_v = lambda buf: buf[:].rearrange("p (a c) l -> p a c l", c=2)

        def gate_col(row, chunk, head):
            return dng[:, row, chunk, bass.ds(head, 1)]

        def q4(bank, p):
            return bank[:, P * p:P * p + P]

        def blocks(tile, k):
            return tile.rearrange("p (n h s) -> p n h s", h=2, s=1 << k)

        def blocks4(tiles, k):
            return tiles[:].rearrange("p q (n h s) -> p q n h s", h=2, s=1 << k)

        def half4(bank, k):
            return bank[:, 0:2 * P].rearrange("p (q n s) -> p q n s", q=4, s=1 << k)

        def convolved(mm, i):
            return cq[:] if mm == 0 else pr[:, bass.ds(HT * mm + 2 * i, 2)]

        def deltanet_act(act):
            act.wait_ge(grp_done, glu_end)
            act.activation(dng[:, BETA], ba[:, :, 0:HT], ACT.Tanh, scale=0.5).then_inc(dna_set.sem, 1)
            act.activation(dng[:, EALOG, 0], dnb[:, 0], ACT.Exp).then_inc(dna_set.sem, 1)
            act.wait_ge(dnd_set.sem, dnd_set.at(0, "pre"))
            act.activation(dng[:, EABS], dng[:, EABS], ACT.Exp, scale=-1.0).then_inc(dna_set.sem, 1)
            act.wait_ge(dna_set.sem, dna_set.at(0, "eabs"))
            act.activation(dng[:, EABS], dng[:, EABS], ACT.Ln, bias=consts[:, 4:5]).then_inc(dna_set.sem, 1)
            act.wait_ge(dnd_set.sem, dnd_set.at(0, "arg"))
            act.activation(dng[:, EG], dng[:, GCUM], ACT.Exp).then_inc(dna_set.sem, 1)
            act.activation(dng[:, TAIL], dng[:, TAIL], ACT.Exp).then_inc(dna_set.sem, 1)

            with act.Fori(0, HT // 2) as i:
                def done(ins):
                    ins.then_inc(dna.sem, 1)

                def on(steps, name):
                    act.wait_ge(steps.sem, steps.at(i, name))

                for other in (dnd, dne, dnp):
                    act.wait_ge(other.sem, other.begin(i))
                on(dnc, "c23")
                for mm, dst in enumerate((sq[:], pair_v(d), pair_v(dt))):
                    done(act.activation(dst, convolved(mm, i), ACT.Tanh, scale=0.5))
                on(dnd, "sl1")
                done(act.activation(sq[:], cv[:, 0:2], ACT.Square))
                done(act.activation(pair_v(mb), cv[:, 2:4], ACT.Square))
                on(dne, "nq")
                done(act.activation(sq[:], pa[:].rearrange("p (a l) -> p a l", a=2), ACT.Ln, scale=0.25, bias=consts[:, 3:4]))
                on(dne, "nk")
                done(act.activation(pair_v(mb), pb[:].rearrange("p (a l) -> p a l", a=2), ACT.Ln, scale=0.25, bias=consts[:, 3:4]))
                act.wait_ge(dna.sem, dna.at(i, "lnk"))
                done(act.activation(sq[:], sq[:], ACT.Exp, scale=-0.5))
                done(act.activation(mb[:], mb[:], ACT.Exp, scale=-0.5))
                on(dnd, "nk")
                done(act.activation(sq[:], pr[:, bass.ds(4 * HT + 2 * i, 2)], ACT.Tanh, scale=0.5))
                on(dnd, "dm")
                done(act.activation(pp[:], dt[:], ACT.Exp))
                on(dne, "vt")
                done(act.activation(vt[:], pgf[:, 2].rearrange("p (q l) -> p q l", q=4), ACT.Copy, scale=0.5))
                on(dne, "kt")
                act.activation(kt[:, 0], q4(pgf[:, 3], 0), ACT.Copy, scale=gate_col(TAIL, 0, 2 * i))
                done(act.activation(kt[:, 1], q4(pgf[:, 3], 1), ACT.Copy, scale=gate_col(TAIL, 0, 2 * i + 1)))
                for k in range(LEVELS):
                    on(dne, f"p{k}")
                    if k == 0:
                        on(dnd, "am")
                    done(act.activation(pp[:], pa[:].rearrange("p (q l) -> p q l", q=4), ACT.Copy))
                on(dne, "vn0")
                done(act.activation(prob_v(vn)[:, :, 0], pgf[:, 0, 0:2 * P].rearrange("p (a l) -> p a l", a=2), ACT.Copy))
                on(dne, "S")
                done(act.activation(sst[:], pgf[:, 1, 0:2 * P].rearrange("p (a l) -> p a l", a=2), ACT.Copy))
                on(dne, "vn1")
                done(act.activation(prob_v(vn)[:, :, 1], pgf[:, 3, 0:2 * P].rearrange("p (a l) -> p a l", a=2), ACT.Copy))
                on(dne, "ov")
                done(act.activation(pp[:], pa[:].rearrange("p (q l) -> p q l", q=4), ACT.Copy))
                on(dnd, "o1")
                for p in range(4):
                    last = act.activation(vt[:, p], pp[:, p], ACT.Square, accum_out=dng[:, SUMSQ, 0, p:p + 1])
                done(last)
                act.wait_ge(dna.sem, dna.at(i, "ss"))
                done(act.activation(dng[:, SUMSQ, 0, 0:4], dng[:, SUMSQ, 0, 0:4], ACT.Sqrt, scale=1.0 / P, bias=consts[:, 0:1]))
                on(dnd, "yz")
                done(act.activation(ahi[:, bass.ds(2 * i, 2)], sq[:], ACT.Copy, scale=0.5))

        def deltanet_dve(dve, link, ada_unit, ada_take):
            dve.wait_ge(grp_done, glu_end)
            dve.wait_ge(dna_set.sem, dna_set.at(0, "ealog"))
            link(dve.tensor_scalar(dng[:, BETA], dng[:, BETA], 0.5, 0.5, ALU.mult, ALU.add))
            link(dve.tensor_tensor(dng[:, XA], ba[:, :, HT:2 * HT], over(dnb[:, 1], 2), ALU.add))
            dve.scalar_tensor_tensor(dng[:, EABS], dng[:, XA], -1.0, dng[:, XA], ALU.mult, ALU.max).then_inc(dnd_set.sem, 1)
            dve.wait_ge(dna_set.sem, dna_set.at(0, "ln"))
            link(dve.scalar_tensor_tensor(dng[:, XA], dng[:, XA], 0.0, dng[:, EABS], ALU.max, ALU.add))
            dve.scalar_tensor_tensor(dng[:, GDEC], dng[:, XA], -1.0, over(dng[:, EALOG, 0], 2), ALU.mult,
                                     ALU.mult).then_inc(dnd_set.sem, 1)
            dve.wait_ge(dne_set.sem, 1)
            link(dve.tensor_copy(dng[:, GCUM], pb[:, 0:2 * HT].rearrange("p (c h) -> p c h", c=2)))
            dve.tensor_tensor(dng[:, TAIL], pb[:, 2 * HT:4 * HT].rearrange("p (c h) -> p c h", c=2), dng[:, GCUM],
                              ALU.subtract).then_inc(dnd_set.sem, 1)
            dve.wait_ge(dna_set.sem, dna_set.at(0, "eG"))
            dve.tensor_tensor(dng[:, BEG], dng[:, BETA], dng[:, EG], ALU.mult).then_inc(dnd_set.sem, 1)
            dve.wait_ge(dnd_set.sem, dnd_set.at(0, "done"))

            dve.wait_ge(dnp_set.sem, 1)

            def convolve(i, n):
                mm, tap = n // 4, n % 4
                dve.wait_ge(dnc.sem, dnc.begin(i) + n)
                for a in range(2):
                    src = pr[:, bass.ds(HT * (mm + 1) + a + 2 * i, 1)]
                    w = dcw[:, bass.ds(3 * HT * (3 - tap) + HT * mm + a + 2 * i, 1)]
                    dst = cq[:, a:a + 1] if mm == 0 else pr[:, bass.ds(HT * mm + a + 2 * i, 1)]
                    if tap == 0:
                        last = dve.tensor_scalar(dst, src, w, None, ALU.mult)
                    else:
                        last = dve.scalar_tensor_tensor(dst[:, :, tap:], src[:, :, 0:L - tap], w, dst[:, :, tap:],
                                                        ALU.mult, ALU.add)
                last.then_inc(dnc.sem, 1)

            for n in range(12):
                convolve(0, n)

            def dve_round(i):
                def done(ins):
                    ins.then_inc(dnd.sem, 1)

                def on(steps, name):
                    dve.wait_ge(steps.sem, steps.at(i, name))

                for other in (dna, dne, dnp):
                    dve.wait_ge(other.sem, other.begin(i))
                for p in range(4):
                    last = dve.tensor_scalar(rr[:, p], tri[:], gate_col(GDEC, p % 2, 2 * i + p // 2), None, ALU.mult)
                done(last)
                for p in range(4):
                    last = dve.tensor_scalar(vt[:, p], ident[:], gate_col(BETA, p % 2, 2 * i + p // 2), None, ALU.mult)
                done(last)
                for mm, th in enumerate((sq[:], pair_v(d), pair_v(dt))):
                    on(dna, f"th{mm}")
                    done(dve.scalar_tensor_tensor(cv[:, 2 * mm:2 * mm + 2], th, 1.0, convolved(mm, i), ALU.add, ALU.mult))
                on(dna, "stq")
                done(dve.scalar_tensor_tensor(cv[:, 0:2], cv[:, 0:2], 0.5 * P ** -0.5, sq[:], ALU.mult, ALU.mult))
                on(dna, "stk")
                done(dve.scalar_tensor_tensor(cv[:, 2:4], cv[:, 2:4], 0.5, pair_v(mb), ALU.mult, ALU.mult))
                on(dnd, "sl2")
                on(dne, "gi")
                for p in range(4):
                    last = dve.tensor_scalar(dt[:, p], q4(pc, p), gate_col(GCUM, p % 2, 2 * i + p // 2), 0.0,
                                             ALU.subtract, ALU.min)
                done(last)
                on(dna, "ed")
                on(dne, "gram")
                v4 = lambda bank: bank.rearrange("p (q l) -> p q l", q=4)
                done(dve.tensor_tensor(m[:], v4(pgf[:, 0]), pp[:], ALU.mult))
                on(dne, "bi")
                on(dnd, "m0")
                done(dve.scalar_tensor_tensor(m[:], m[:], -1.0, v4(pb[:]), ALU.mult, ALU.mult))
                done(dve.tensor_tensor(at[:], v4(pgf[:, 1]), pp[:], ALU.mult))
                on(dna, "vt")
                for p in range(4):
                    last = dve.tensor_scalar(rr[:, p], vt[:, p], gate_col(BETA, p % 2, 2 * i + p // 2), None, ALU.mult)
                done(last)
                ab = by_name["glu"]["ab1"] + 2 * i
                on(dnp, "init")
                for k in range(LEVELS):
                    if k < LEVELS - 1:
                        on(dne, f"y{k}")
                        even = blocks4(d, k)[:, :, :, 0]
                        done(dve.tensor_tensor(even, even, half4(pc, k), ALU.add))
                    on(dne, f"x{k}")
                    odd = blocks4(dt, k)[:, :, :, 1]
                    done(dve.tensor_tensor(odd, odd, half4(pb, k), ALU.add))
                    if not (isinstance(i, int) and i == HT // 2 - 1):
                        for n in range(12 * k // LEVELS, 12 * (k + 1) // LEVELS):
                            convolve(i + 1, n)
                    ada_unit(ab + k // 4, k % 4, k // 4, before=2 * ADA_FIRST + 2)
                ada_unit(ab + 1, 3, 1, before=2 * ADA_FIRST + 2)
                on(dne, "kS")
                for a in range(2):
                    last = dve.tensor_scalar(vt[:, 2 * a], q4(pgf[:, 2], a), gate_col(BEG, 1, 2 * i + a), None, ALU.mult)
                done(last)
                on(dnd, "r1a")
                done(dve.tensor_tensor(prob_v(rr)[:, :, 1], prob_v(rr)[:, :, 1], prob_v(vt)[:, :, 0], ALU.subtract))
                ada_take(ab)
                on(dna, "oc")
                on(dne, "qS")
                for a in range(2):
                    last = dve.scalar_tensor_tensor(pp[:, 2 * a + 1], q4(pb, a), gate_col(EG, 1, 2 * i + a), pp[:, 2 * a + 1],
                                                    ALU.mult, ALU.add)
                done(last)
                on(dna, "rs")
                done(dve.reciprocal(dng[:, SUMSQ, 0, 0:4], dng[:, SUMSQ, 0, 0:4]))
                on(dnd, "rmsr")
                for p in range(4):
                    last = dve.tensor_scalar(pp[:, p], pp[:, p], dng[:, SUMSQ, 0, p:p + 1], None, ALU.mult)
                done(last)
                z = pr[:, bass.ds(4 * HT + 2 * i, 2)]
                done(dve.scalar_tensor_tensor(sq[:], sq[:], 1.0, z, ALU.add, ALU.mult))
                ada_take(ab + 1)
                on(dne, "turn")
                on(dnd, "zs")
                done(dve.scalar_tensor_tensor(sq[:], pc[:].rearrange("p (a l) -> p a l", a=2), misc[:, 48:49], sq[:],
                                              ALU.mult, ALU.mult))
                on(dna, "hi")
                done(dve.scalar_tensor_tensor(alo[:, bass.ds(2 * i, 2)], sq[:], 0.5, ahi[:, bass.ds(2 * i, 2)].bitcast(F32),
                                              ALU.mult, ALU.subtract))

            bodies(dve, HT // 2, dve_round, peel=True)

        def deltanet_pe(pe, ada_sum):
            pe.wait_ge(dnp_set.sem, 1)
            pe.wait_ge(dnd_set.sem, dnd_set.at(0, "g"))
            for n, w in enumerate((tri, ones)):
                for chunk in range(2):
                    last = pe.matmul(pb[:, HT * (2 * n + chunk):HT * (2 * n + chunk + 1)], w[:], dng[:, GDEC, chunk],
                                     start=True, stop=True)
            last.then_inc(dne_set.sem, 1)
            pe.wait_ge(dnd_set.sem, dnd_set.at(0, "arg"))

            with pe.Fori(0, HT // 2) as i:
                def done(ins):
                    ins.then_inc(dne.sem, 1)

                def on(steps, name):
                    pe.wait_ge(steps.sem, steps.at(i, name))

                def each(bank, pairs):
                    for n, (a, b) in enumerate(pairs):
                        last = pe.matmul(q4(bank, n), a, b, start=True, stop=True)
                    done(last)

                def each_half(bank, pairs):
                    for n, (a, b) in enumerate(pairs):
                        last = pe.matmul(bank[:, P // 2 * n:P // 2 * n + P // 2], a, b, start=True, stop=True)
                    done(last)

                def turn(bank, sources):
                    for n, a in enumerate(sources):
                        last = pe.transpose(q4(bank, n), a, ident[:])
                    done(last)

                def part(tile, chunk):
                    return cv[:, tile, P * chunk:P * chunk + P]

                problems = [(p // 2, p % 2) for p in range(4)]
                on(dnd, "gt")
                done(pe.matmul(pc[:], ones[:], rr[:], start=True, stop=True))
                on(dna, "sqq")
                done(pe.matmul(pa[:], ones[:], sq[:], start=True, stop=True))
                on(dna, "sqk")
                done(pe.matmul(pb[:], ones[:], mb[:], start=True, stop=True))
                on(dnd, "nk")
                for n, (a, chunk) in enumerate(problems):
                    pe.matmul(q4(pgf[:, 0], n), part(2 + a, chunk), part(2 + a, chunk), start=True, stop=True)
                each(pgf[:, 1], [(part(2 + a, chunk), part(a, chunk)) for a, chunk in problems])
                on(dnd, "bt")
                done(pe.matmul(pb[:], ones[:], vt[:], start=True, stop=True))
                turn(pgf[:, 2], [part(4 + a, chunk) for a, chunk in problems])
                turn(pgf[:, 3], [part(2 + a, 0) for a in range(2)])
                on(dnp, "init")
                for k in range(LEVELS):
                    on(dnp, f"mb{k}")
                    if k:
                        on(dnd, f"d{k - 1}")
                    each(pa, [(mb[:, p], d[:, p]) for p in range(4)])
                    on(dna, f"p{k}")
                    if k == 0:
                        on(dnd, "m1")
                    if k:
                        on(dnd, f"dt{k - 1}")
                    if k < LEVELS - 1:
                        each_half(pc, [(dt[:, p], blocks(pp[:, p], k)[:, :, 0]) for p in range(4)])
                    each_half(pb, [(pp[:, p], blocks(dt[:, p], k)[:, :, 1]) for p in range(4)])
                on(dnd, f"dt{LEVELS - 1}")
                on(dnd, "r0")
                on(dna, "kt")
                each(pgf[:, 0], [(dt[:, 2 * a], rr[:, 2 * a]) for a in range(2)])
                on(dna, "vn0")
                on(dnd, "am")
                each(pgf[:, 1], [(kt[:, a], vn[:, 2 * a]) for a in range(2)])
                on(dna, "S")
                each(pgf[:, 2], [(part(2 + a, 1), sst[:, a]) for a in range(2)])
                on(dnd, "r1")
                each(pgf[:, 3], [(dt[:, 2 * a + 1], rr[:, 2 * a + 1]) for a in range(2)])
                ada_sum(by_name["glu"]["ab1"] + 2 * i, 0)
                on(dna, "vn1")
                on(dnp, "at")
                each(pa, [(at[:, p], vn[:, p]) for p in range(4)])
                each(pb, [(part(a, 1), sst[:, a]) for a in range(2)])
                ada_sum(by_name["glu"]["ab1"] + 2 * i + 1, 1)
                on(dnd, "on")
                turn(pc, [pp[:, p] for p in range(4)])

        def deltanet_pool(pool):
            pool.wait_ge(grp_done, glu_end)
            pool.memset(tri[:], 1.0)
            link_pool(pool, pool.memset(lm[:], 0.0))
            link_pool(pool, pool.affine_select(out=tri[:], in_=tri[:], compare_op=ALU.is_ge, fill=0.0, base=0,
                                               pattern=[[1, P]], channel_multiplier=-1))
            for k in range(LEVELS):
                size = 1 << k
                v = lm[:, k].rearrange("p (n h s) -> p n h s", h=2, s=size)[:, :, 1]
                link_pool(pool, pool.affine_select(out=v, in_=v, compare_op=ALU.is_gt, fill=1.0, base=0,
                                                   pattern=[[2 * size, P // (2 * size)], [0, size]], channel_multiplier=-1))
                link_pool(pool, pool.affine_select(out=v, in_=v, compare_op=ALU.is_gt, fill=0.0, base=size,
                                                   pattern=[[2 * size, P // (2 * size)], [0, size]], channel_multiplier=-1))
            pool.sem_inc(dnp_set.sem, 1)
            with pool.Fori(0, HT // 2) as i:
                def done(ins):
                    ins.then_inc(dnp.sem, 1)

                def on(steps, name):
                    pool.wait_ge(steps.sem, steps.at(i, name))

                on(dna, "ed")
                carry(pool)
                pool.tensor_copy(d[:], ident[:].unsqueeze(1).broadcast_to([P, 4, P]))
                done(pool.tensor_copy(dt[:], ident[:].unsqueeze(1).broadcast_to([P, 4, P])))
                on(dnd, "m1")
                for k in range(LEVELS):
                    if k:
                        on(dne, f"p{k - 1}")
                    done(pool.tensor_tensor(mb[:], m[:], lm[:, k].unsqueeze(1).broadcast_to([P, 4, P]), ALU.mult))
                on(dnd, "am")
                done(pool.tensor_tensor(at[:], at[:], tri[:].unsqueeze(1).broadcast_to([P, 4, P]), ALU.mult))

        GB, GC, XC, Q, K, V = (HT * n for n in range(6))
        SLOPE, MAXES, SUMS, NEGLAM, LAMS = 0, 4, 8, 12, 13
        MQ = 51

        def attention_act(act):
            act.wait_ge(tile_used, by_name["out1"]["u0"])
            for q in range(2):
                act.wait_ge(scd.sem, scd.at(4 * q + 3, "g"))
                act.activation(ahi[:, 4 * q:4 * q + 4], pr1[:, 4 * q:4 * q + 4], ACT.Copy).then_inc(sc_hi, 1)
            act.wait_ge(da_sete.sem, 1)
            act.activation(dav[:, LAMS:LAMS + 2], pm[:, 0:2], ACT.Exp).then_inc(da_seta.sem, 1)
            with act.Fori(0, DA_HEADS) as h:
                def done(ins):
                    ins.then_inc(daa.sem, 1)

                def on(steps, name):
                    act.wait_ge(steps.sem, steps.at(h, name))

                on(dae_, "vt")
                done(act.activation(davt[:].rearrange("p a l -> p (a l)"), pgf[:, 2], ACT.Copy))
                for b in range(2):
                    w = P * (b + 1)
                    on(dad, f"ng{b}")
                    for mp in range(2):
                        last = act.activation(das[:, mp, 0:w], das[:, mp, 0:w], ACT.Exp,
                                              bias=dav[:, MAXES + mp:MAXES + mp + 1],
                                              accum_out=dav[:, SUMS + mp:SUMS + mp + 1])
                    done(last)
                    on(dae_, f"ct{b}")
                    done(act.activation(dact[:, b:2 * b + 1].rearrange("p k l -> p (k l)"),
                                        pgf[:, 3, P * b:P * b + w], ACT.Copy))
                on(dae_, "pv1")
                done(act.activation(dao[:].rearrange("p a l -> p (a l)"), pa[:], ACT.Copy))
                done(act.activation(das[:].rearrange("p a l -> p (a l)"), pa[:], ACT.Square))
                on(dae_, "ss")
                done(act.activation(dac[:], pb[:, 0:L], ACT.Sqrt, scale=1.0 / (2 * P), bias=consts[:, 0:1]))

        def short_conv(dve, t):
            def step(name, ins):
                ins.then_inc(scd.sem, 1)
                dve.wait_ge(scd.sem, scd.at(t, name))

            mm, cc, gb = scm[:, 0:1], scv[:, 0:1], pr1[:, bass.ds(GB + t, 1)]
            dve.wait_ge(scd.sem, scd.begin(t))
            step("m", dve.tensor_tensor(mm, pr1[:, bass.ds(GC + t, 1)], pr1[:, bass.ds(XC + t, 1)], ALU.mult))
            step("c0", dve.tensor_scalar(cc, mm, misc[:, bass.ds(16 + 2 * HT + t, 1)], None, ALU.mult))
            for tap in (1, 2):
                step(f"c{tap}", dve.scalar_tensor_tensor(cc[:, :, tap:], mm[:, :, 0:L - tap],
                                                         misc[:, bass.ds(16 + (2 - tap) * HT + t, 1)], cc[:, :, tap:],
                                                         ALU.mult, ALU.add))
            dve.tensor_tensor(gb, cc, gb, ALU.mult).then_inc(scd.sem, 1)

        def attention_dve(dve):
            for q in range(2):
                k = slice(4 * q, 4 * q + 4)
                dve.wait_ge(sc_hi, q + 1)
                dve.tensor_tensor(alo[:, k], pr1[:, k], ahi[:, k].bitcast(F32), ALU.subtract).then_inc(sc_lo, 1)
            dve.wait_ge(grp_done, by_name["in1"]["g0"] + 12 + 2)
            dve.tensor_tensor(dav[:, LAMS:LAMS + 2], misc[:, MQ:MQ + 3:2], misc[:, MQ + 1:MQ + 4:2],
                              ALU.mult).then_inc(da_setd.sem, 1)
            dve.wait_ge(da_seta.sem, 1)
            dve.scalar_tensor_tensor(dav[:, NEGLAM:NEGLAM + 1], dav[:, LAMS + 1:LAMS + 2], -LAMBDA_INIT, dav[:, LAMS:LAMS + 1],
                                     ALU.add, ALU.subtract).then_inc(da_setd.sem, 1)
            dve.wait_ge(da_setd.sem, da_setd.at(0, "lam"))
            dve.wait_ge(da_setp.sem, 1)
            with dve.Fori(0, DA_HEADS) as h:
                def done(ins):
                    ins.then_inc(dad.sem, 1)

                def on(steps, name):
                    dve.wait_ge(steps.sem, steps.at(h, name))

                for other in (daa, dae_):
                    dve.wait_ge(other.sem, other.begin(h))
                dve.wait_ge(dad.sem, dad.begin(h))
                done(dve.tensor_scalar(daq[:], pr1[:, bass.ds(Q + 2 * h, 2)], P ** -0.5, None, ALU.mult))
                done(dve.tensor_copy(dao[:], pr1[:, bass.ds(V + 2 * h, 2)]))
                for b in range(2):
                    w = P * (b + 1)
                    on(dae_, f"sc{b}")
                    if b:
                        on(dad, "c0")
                    dist = dand[:, P * b:P * b + w].unsqueeze(1).broadcast_to([P, 2, w])
                    done(dve.scalar_tensor_tensor(das[:, :, 0:w], dist, dav[:, bass.ds(SLOPE + h, 1)],
                                                  pgf[:, b].rearrange("p (m l) -> p m l", m=2)[:, :, 0:w],
                                                  ALU.mult, ALU.add))
                    on(dad, f"s{b}")
                    done(dve.tensor_reduce(dav[:, MAXES:MAXES + 2], das[:, :, 0:w], AX_X, ALU.max))
                    on(dad, f"mx{b}")
                    done(dve.tensor_scalar(dav[:, MAXES:MAXES + 2], dav[:, MAXES:MAXES + 2], -1.0, None, ALU.mult))
                    on(daa, f"e{b}")
                    done(dve.reciprocal(dav[:, SUMS:SUMS + 2], dav[:, SUMS:SUMS + 2]))
                    on(dad, f"r{b}")
                    done(dve.tensor_tensor(dav[:, SUMS + 1:SUMS + 2], dav[:, SUMS + 1:SUMS + 2],
                                           dav[:, NEGLAM:NEGLAM + 1], ALU.mult))
                    on(dad, f"rl{b}")
                    if b:
                        on(dae_, "ct0")
                    done(dve.tensor_scalar(dac[:, 0:w], das[:, 1, 0:w], dav[:, SUMS + 1:SUMS + 2], None, ALU.mult))
                    on(dad, f"t{b}")
                    done(dve.scalar_tensor_tensor(dac[:, 0:w], das[:, 0, 0:w], dav[:, SUMS:SUMS + 1], dac[:, 0:w],
                                                  ALU.mult, ALU.add))
                on(daa, "std")
                done(dve.reciprocal(dac[:], dac[:]))
                on(dad, "rr")
                done(dve.tensor_tensor(dao[:], dao[:], over(dac[:], 2), ALU.mult))
                on(dad, "on")
                for f in range(2):
                    last = dve.tensor_scalar(dao[:, f], dao[:, f], misc[:, 49 + f:50 + f], 1.0 - LAMBDA_INIT,
                                             ALU.mult, ALU.mult)
                done(last)
                on(dad, "og")
                where = bass.ds(HT + 2 * h, 2)
                done(dve.tensor_copy(ahi[:, where], dao[:]))
                on(dad, "hi")
                done(dve.tensor_tensor(alo[:, where], dao[:], ahi[:, where].bitcast(F32), ALU.subtract))

        def attention_pe(pe):
            pe.wait_ge(grp_done, by_name["in1"]["g0"] + 12 + 2)
            pe.wait_ge(da_setd.sem, da_setd.at(0, "prod"))
            pe.matmul(pm[:, 0:2], ones[:], dav[:, LAMS:LAMS + 2], start=True, stop=True).then_inc(da_sete.sem, 1)
            with pe.Fori(0, DA_HEADS) as h:
                def done(ins):
                    ins.then_inc(dae_.sem, 1)

                def on(steps, name):
                    pe.wait_ge(steps.sem, steps.at(h, name))

                on(dad, "q")
                for b in range(2):
                    w = P * (b + 1)
                    for mp in range(2):
                        last = pe.matmul(pgf[:, b, L * mp:L * mp + w], daq[:, mp, P * b:P * b + P],
                                         pr1[:, bass.ds(K + 2 * h + mp, 1), 0:w], start=True, stop=True)
                    done(last)
                on(dad, "v")
                for chunk in range(2):
                    for f in range(2):
                        last = pe.transpose(q4(pgf[:, 2], 2 * chunk + f), dao[:, f, P * chunk:P * chunk + P], ident[:])
                done(last)
                for b in range(2):
                    on(dad, f"c{b}")
                    for n in range(b + 1):
                        last = pe.transpose(q4(pgf[:, 3], b + n), dac[:, P * n:P * n + P], ident[:])
                    done(last)
                    on(daa, f"ct{b}")
                    for f in range(2):
                        for n in range(b + 1):
                            last = pe.matmul(pa[:, L * f + P * b:L * f + P * b + P], davt[:, n, P * f:P * f + P],
                                             dact[:, b + n], start=(n == 0), stop=(n == b))
                    done(last)
                on(daa, "sq")
                for f in range(2):
                    last = pe.matmul(pb[:, 0:L], ones[:], das[:, f], start=(f == 0), stop=(f == 1))
                done(last)

        def attention_pool(pool):
            pool.wait_ge(act_ready, 12)
            pool.iota(dand[:, 0:P], [[1, P]], base=0, channel_multiplier=-1, allow_small_or_imprecise_dtypes=True)
            link_pool(pool, pool.iota(dand[:, P:3 * P], [[1, L]], base=-P, channel_multiplier=-1,
                                      allow_small_or_imprecise_dtypes=True))
            for h in range(DA_HEADS):
                pool.memset(dav[:, SLOPE + h:SLOPE + h + 1], 2.0 ** (-8.0 * (h + 1) / DA_HEADS))
            pool.affine_select(out=dand[:, 0:P], in_=dand[:, 0:P], compare_op=ALU.is_ge, fill=BIG, base=0,
                               pattern=[[-1, P]], channel_multiplier=1)
            pool.affine_select(out=dand[:, P:3 * P], in_=dand[:, P:3 * P], compare_op=ALU.is_ge, fill=BIG, base=P,
                               pattern=[[-1, L]], channel_multiplier=1).then_inc(da_setp.sem, 1)

        def link_pool(pool, ins):
            pool_links[0] += 1
            ins.then_inc(pool_chain, 1)
            pool.wait_ge(pool_chain, pool_links[0])

        def carry(pool):
            pool.tensor_tensor(pidle[:, 1:2], pidle[:, 0:1], pidle[:, 0:1], ALU.add)

        block = ctx.enter_context(nc.Block())

        def bodies(engine, n, body, peel=False):
            if n == 1:
                body(0)
            elif peel:
                with engine.Fori(0, n - 1) as i:
                    body(i)
                body(n - 1)
            else:
                with engine.Fori(0, n) as i:
                    body(i)

        def ada_source(ab0):
            layer = min(ab0 // LAYER_BLOCKS, DEPTH - 1)
            return ada_w[layer], (ab0 - layer * LAYER_BLOCKS) * GROUP

        def mod_cols(n):
            base = n * 3 * KT
            return base, base + KT, base + 2 * KT, 12 * n + 8, 12 * n + 12

        def load_ada(engine, landed, src, col, ab, j):
            engine.wait_ge(ada_step, 16 * ab + (4 * j + ADA_FREE - 4))
            engine.dma_start(aw[:, j % 2], src[UK * P * j:UK * P * (j + 1), bass.ds(col, GROUP)]
                             .rearrange("(k p) n -> p k n", p=P)).then_inc(landed[j % 2], 16)

        @block.sync
        def _(sp):
            def load(dst, src, s):
                sp.dma_start(dst, src).then_inc(s, 16)

            for layer in range(DEPTH):
                load(vrow[0:N_ADA, layer], ada_b[layer].rearrange("(t p) -> t p", p=P), vec_in)
            for n, v in enumerate((ln1_g, ln1_b, ln2_g, ln2_b)):
                load(vrow[32 * n:32 * n + 32, 2], v.rearrange("l (t p) -> (l t) p", p=P), vec_in)
            load(vrow[0:96, 3], dn_conv_w[0].rearrange("k (t p) -> (k t) p", p=P), vec_in)
            load(vrow[0:16, 4], c[0].rearrange("(t p) -> t p", p=P), vec_in)
            load(vrow[16:40, 4], sc_conv_w[0].rearrange("k (t p) -> (k t) p", p=P), vec_in)
            load(vrow[40:48, 4], s5_d[0].rearrange("(t g) c -> t (g c)", t=HT), vec_in)
            load(vrow[48:49, 4], dn_norm_g, vec_in)
            load(vrow[49:51, 4], da_norm_g.rearrange("a (t p) -> (a t) p", p=P), vec_in)
            for n, v in enumerate((da_lq1, da_lk1, da_lq2, da_lk2)):
                load(vrow[51 + n:52 + n, 4], v, vec_in)
            load(vrow[0:32, 5], s5_a_re[0].rearrange("(t g) s -> t (g s)", g=2), vec_in)
            load(vrow[32:64, 5], s5_a_im[0].rearrange("(t g) s -> t (g s)", g=2), vec_in)
            load(vrow[64:96, 6, 0:2], s5_log_dt[0].rearrange("(t g) -> t g", g=2), vec_in)
            load(xrow[:], x[0].rearrange("(t p) d -> p t d", p=P), x_in)
            def ada_first(i):
                for n in range(FIRST_SLOTS):
                    j, b = n // 2, n % 2
                    sp.wait_ge(ada_step, 32 * i + 8 * j + 5)
                    sp.dma_start(first_slots[n], ada_w[0][UK * P * j:UK * P * (j + 1), bass.ds(GROUP * (2 * i + b), GROUP)]
                                 .rearrange("(k p) n -> p k n", p=P)).then_inc(ada_in_first[n], 16)

            bodies(sp, ADA_FIRST, ada_first)
            load(wba[:], ab_w_in[0][:, AB_SMALL:AB_SMALL + N_SMALL].rearrange("(k p) n -> p k n", p=P), par_in)
            load(dnb[:, 0], dn_a_log.broadcast_to([P, HT]), par_in)
            load(dnb[:, 1], dn_dt_bias.broadcast_to([P, HT]), par_in)
            for dst, src in ((s5br, s5_b_re), (s5bi, s5_b_im)):
                load(dst[:], src[0].rearrange("(t g) s c -> (g s) t c", g=2), par_in)
            for dst, src in ((s5cr, s5_c_re), (s5ci, s5_c_im)):
                load(dst[:], src[0].rearrange("(t g) c s -> (g c) t s", t=HT), par_in)

            def weight_unit(p, i, j):
                w, first, step = p["groups"][j // p["units"]]
                k = (p["k0"] + UK * (j % p["units"])) * P
                sp.wait_ge(lo_done, p["u0"] + j + p["bu"] * i + 1)
                sp.dma_start(raw[:, j % 4], w[k:k + UK * P, bass.ds(first + step * i, GROUP)]
                             .rearrange("(k p) n -> p k n", p=P)).then_inc(raw_in[j % 4], 16)

            for p in products:
                def body(i, p=p, ahead=0):
                    for j in range(ahead, p["bu"]):
                        weight_unit(p, i, j)
                if p["name"] == "out0":
                    for j in range(4):
                        weight_unit(p, 0, j)
                    ab1 = by_name["glu"]["ab1"]
                    src, col0 = ada_source(ab1)

                    def ada_round(i):
                        for n in range(8):
                            b, q = n // 4, n % 4
                            load_ada(sp, ada_in, src, col0 + GROUP * b + 2 * GROUP * i, ab1 + b + 2 * i, q)
                    bodies(sp, HT // 2, ada_round)
                    body(0, ahead=4)
                    body(1)
                else:
                    bodies(sp, p["bodies"], body)

            for b in range(2):
                sp.wait_ge(o_taken, 4 * b + 4)
                sp.dma_start(out[0, b * P:(b + 1) * P, :], orow[:, b]).then_inc(out_done, 16)
            sp.wait_ge(out_done, 32)

        @block.scalar
        def _(act):
            def split_hi(j):
                act.activation(whi[:, j % 2], raw[:, (j + 2) % 4], ACT.Copy).then_inc(hi_done, 1)

            def product(p, evacuate, before=None, after=None):
                def body(i):
                    for j in range(p["bu"]):
                        u = p["u0"] + p["bu"] * i + j
                        static = p["bodies"] == 1
                        if before:
                            before(i, j)
                        if not (static and u + 2 >= n_units):
                            act.wait_ge(raw_in[(j + 2) % 4], 16 * ((j + 2) // 4 + 1) + (16 * (p["u0"] // 4))
                                        + 16 * (p["bu"] // 4) * i)
                            act.wait_ge(tile_used, u + 1)
                            split_hi(j)
                        if (j + 1) % p["units"] == 0 and evacuate:
                            evacuate(i, j // p["units"], u + 1)
                        if after:
                            after(i, j)
                bodies(act, p["bodies"], body, peel=before is not None)

            def take(dst):
                def evacuate(i, g, units):
                    act.wait_ge(tile_used, units)
                    act.activation(dst(i, g), pg[:, g % 2], ACT.Copy).then_inc(grp_done, 1)
                return evacuate

            def ffn(layer):
                for n, (first, groups) in enumerate(FFN_BLOCKS):
                    p = by_name[f"up{layer}{n}"]

                    def up(i, g, units, p=p):
                        if g == 0:
                            act.wait_ge(tile_used, units)
                            act.wait_ge(grp_done, p["g0"] + 2 * i + 2)
                            act.activation(gt[:], pg[:, 0], ACT.Tanh, scale=0.5).then_inc(gate_t, 1)
                        else:
                            act.wait_ge(grp_done, p["g0"] + 2 * i + 2 + 2)
                            act.activation(hhi[:, bass.ds(GT * i, GT)], gs[:], ACT.Copy).then_inc(hid_hi, 1)
                    product(p, up)
                    p = by_name[f"down{layer}{n}"]
                    product(p, None)

            def split_h(n, q):
                for t in range(4 * q, 4 * q + 4):
                    last = act.activation(ahi[:, t], xT[:, t], ACT.Identity, scale=fold[:, 0, t:t + 1],
                                          bias=fold[:, 1, t:t + 1])
                last.then_inc(h_hi, 1)

            def layer_norm(n):
                act.wait_ge(ln_sum, n + 1)
                act.activation(st[:, 0], pa[:, 0:L], ACT.Copy, scale=1.0 / D).then_inc(ln_mean, 1)
                for q in range(4):
                    act.wait_ge(ln_c, 4 * n + q + 1)
                    act.activation(y[:, 4 * q:4 * q + 4], xT[:, 4 * q:4 * q + 4], ACT.Square).then_inc(ln_sq, 1)
                act.wait_ge(ln_var, n + 1)
                act.activation(st[:, 1], pb[:, 0:L], ACT.Sqrt, scale=1.0 / D, bias=consts[:, 0:1]).then_inc(ln_std, 1)
                if n < 3:
                    for q in range(4):
                        act.wait_ge(ln_n, 4 * n + q + 1)
                        split_h(n + 1, q)
                for q in range(4):
                    if n < 3:
                        act.wait_ge(h_ready, 4 * (n + 1) + q + 1)
                    else:
                        act.wait_ge(ln_n, 4 * n + q + 1)
                    for t in range(4 * q, 4 * q + 4):
                        g = (n % 2) * 2 * 32 + (n // 2) * KT + t
                        gain, bias = (fold[:, 2, t:t + 1], fold[:, 3, t:t + 1]) if n < 3 else \
                            (lnc[:, g:g + 1], lnc[:, g + 32:g + 33])
                        last = act.activation(xT[:, t], xT[:, t], ACT.Identity, scale=gain, bias=bias)
                    last.then_inc(ln_gb, 1)

            for steps in (dna, daa):
                act.sem_inc(steps.sem, steps.start)
            act.wait_ge(vec_taken, 6)
            act.activation(cact[:], misc[:, 0:KT], ACT.Tanh, scale=0.5).then_inc(c_tanh, 1)
            act.activation(sv[:, 0], s5c[:, 64:96], ACT.Exp).then_inc(s5_set.sem, 1)
            act.wait_ge(s5_setd.sem, s5_setd.at(0, "x"))
            act.activation(sv[:, 2], sv[:, 1], ACT.Tanh, scale=0.5).then_inc(s5_set.sem, 1)
            act.wait_ge(s5_setd.sem, s5_setd.at(0, "f"))
            act.activation(sv[:, 5], sv[:, 4], ACT.Sin, scale=TWO_PI_LOW)
            act.activation(sv[:, 6], sv[:, 4], ACT.Sin, scale=TWO_PI_LOW / 2).then_inc(s5_set.sem, 1)

            for j in (0, 1):
                act.wait_ge(raw_in[j], 16)
                act.activation(whi[:, j], raw[:, j], ACT.Copy).then_inc(hi_done, 1)
            act.wait_ge(folded, 1)
            for q in range(4):
                split_h(0, q)
            product(by_name["in0u"], take(lambda i, g: pr[:, GT * g:GT * g + GT]))
            act.sem_inc(s5a.sem, s5a.n)

            def s5_input_weights(n):
                act.wait_ge(s5_turned, n + 2)
                act.wait_ge(s5_bu, n + 1)
                act.activation(s5w[:, 0:2], pa[:, 0:2 * P], ACT.Copy).then_inc(s5a.sem, 1)

            def s5_tables(n):
                act.wait_ge(s5p.sem, s5p.at(n + 1, "cosine"))
                act.wait_ge(s5d.sem, s5d.at(n, "p2"))
                act.activation(s5tab[:, 0], s5arg[:, 0], ACT.Sin, scale=TWO_PI_LOW)
                act.activation(s5tab[:, 1], s5arg[:, 1], ACT.Sin, scale=TWO_PI_LOW, bias=consts[:, 1:2])
                act.activation(s5tab[:, 2], s5arg[:, 0], ACT.Sin, scale=-TWO_PI_LOW).then_inc(s5a.sem, 3)

            def s5_output_weights(n):
                act.wait_ge(s5_y, n + 1)
                act.activation(s5w[:, 2], pa[:, 2 * P:3 * P], ACT.Copy).then_inc(s5a.sem, 1)
                act.activation(s5w[:, 3], pa[:, 3 * P:4 * P], ACT.Copy, scale=-1.0).then_inc(s5a.sem, 1)

            def s5_before(i, j):
                n = 8 * i + j + 1
                last = isinstance(n, int) and n == S5_TILES
                if not last:
                    s5_input_weights(n)
                    s5_tables(n)
                if j in (4, 7):
                    t = 2 * i + (j == 7)
                    act.wait_ge(s5gd.sem, s5gd.at(t, "q"))
                    act.activation(s5g[:], s5g[:], ACT.Tanh, scale=math.sqrt(2.0 / math.pi)).then_inc(s5ga.sem, 1)

            def s5_after(i, j):
                n = 8 * i + j + 1
                if not (isinstance(n, int) and n == S5_TILES):
                    s5_output_weights(n)

            s5_input_weights(0)
            s5_tables(0)
            s5_output_weights(0)
            product(by_name["in0"], take(lambda i, g: pr[:, bass.ds(HT + 2 * GT * i + GT * g, GT)]), s5_before, s5_after)
            act.wait_ge(tile_used, by_name["glu"]["u0"])
            for q in range(2):
                act.wait_ge(s5gd.sem, s5gd.at(4 * q + 3, "ys"))
                act.activation(ahi[:, 4 * q:4 * q + 4], pr[:, 4 * q:4 * q + 4], ACT.Copy).then_inc(s5_hi, 1)
            def glu(i, g, units):
                act.wait_ge(tile_used, units)
                act.activation(pg[:, g], pg[:, g], ACT.Tanh, scale=0.5).then_inc(glu_t, 1)
                act.wait_ge(glu_s, g + 1)
                act.activation(ahi[:, HT + GT * g:HT + GT * g + GT], pr[:, GT * g:GT * g + GT], ACT.Copy,
                               scale=0.5).then_inc(glu_hi, 1)
            product(by_name["glu"], glu)
            deltanet_act(act)
            product(by_name["out0"], None)
            layer_norm(0)
            ffn(0)
            layer_norm(1)
            product(by_name["in1"], take(lambda i, g: pr1[:, bass.ds(2 * GT * i + GT * g, GT)]))
            attention_act(act)
            product(by_name["out1"], None)
            layer_norm(2)
            ffn(1)
            layer_norm(3)

        @block.vector
        def _(dve):
            links = [0]

            def link(ins):
                links[0] += 1
                ins.then_inc(chain, 1)
                dve.wait_ge(chain, links[0])

            def ada_unit(ab, j, b, landed=ada_in, before=0):
                dve.wait_ge(landed[j % 2], 32 * (ab - before) + 16 * (j // 2 + 1))
                ada_add(ab, j, b, aw[:, j % 2])

            def ada_add(ab, j, b, unit):
                if j == 0:
                    dve.wait_ge(ada_summed, ab + (1 - b))
                for kk in range(UK):
                    k = UK * j + kk
                    if k == 0:
                        last = dve.tensor_scalar(acc[:, b], unit[:, 0], cact[:, 0:1], None, ALU.mult)
                    else:
                        dve.wait_ge(ada_step, 16 * ab + (k + ADA_FREE))
                        last = dve.scalar_tensor_tensor(acc[:, b], unit[:, kk], cact[:, k:k + 1], acc[:, b],
                                                        ALU.mult, ALU.add)
                    last.then_inc(ada_step, 1)

            def ada_take(ab):
                dve.wait_ge(ada_summed, ab + 2)
                dve.tensor_tensor(mod[:, bass.ds(GT * ab, GT)], pm[:, 0:GT], adab[:, bass.ds(GT * ab, GT)],
                                  ALU.add).then_inc(mod_taken, 1)

            def split_lo(slot, half):
                dve.tensor_tensor(wlo[:, half], raw[:, slot], whi[:, half].bitcast(F32),
                                  ALU.subtract).then_inc(lo_done, 1)

            def product(p, evacuate, before=None, after=None, lag=0, skip_last=False, late=None):
                def body(i, late=None):
                    taken = 0
                    for j in range(p["bu"]):
                        for _ in range(ADA_AT[p["ada"], p["bu"]][j]):
                            ada_unit(p["ab0"] + taken // 4 + p["ada"] * i, taken % 4, taken // 4, ada_in_pool,
                                     2 * ADA_FIRST + (0 if p["name"] == "in0u" else HT))
                            taken += 1
                        u = p["u0"] + p["bu"] * i + j
                        if before:
                            before(i, j)
                        if not (p["bodies"] == 1 and u + 2 >= n_units) and not (skip_last and j == p["bu"] - 1):
                            dve.wait_ge(hi_done, u + 3 - lag)
                            split_lo((j + 2 - lag) % 4, (j - lag) % 2)
                        if (j + 1) % p["units"] == 0 and evacuate:
                            evacuate(i, j // p["units"], u + 1)
                        if j in p["takes"]:
                            ada_take(p["ab0"] + p["takes"][j] + p["ada"] * i)
                        if after:
                            after(i, j)
                        if late:
                            late(j)
                if late:
                    bodies(dve, p["bodies"] - 2, body)
                    bodies(dve, 2, lambda i: body(i + p["bodies"] - 2, lambda j: late(i, j)))
                    return
                bodies(dve, p["bodies"], body, peel=before is not None)

            def ffn(layer):
                for n, (first, groups) in enumerate(FFN_BLOCKS):
                    p = by_name[f"up{layer}{n}"]

                    def up(i, g, units, p=p, done=FFN_GROUPS * layer + first):
                        dve.wait_ge(tile_used, units)
                        if g == 0:
                            dve.wait_ge(gate_t, done + i + 1)
                            dve.scalar_tensor_tensor(gs[:], gt[:], 1.0, pg[:, 0], ALU.add, ALU.mult).then_inc(grp_done, 1)
                        else:
                            dve.wait_ge(grp_done, p["g0"] + 2 * i + 3)
                            dve.scalar_tensor_tensor(gs[:], gs[:], 0.5, pg[:, 1], ALU.mult, ALU.mult).then_inc(grp_done, 1)
                            dve.wait_ge(hid_hi, done + i + 1)
                            dve.tensor_tensor(hlo[:, bass.ds(GT * i, GT)], gs[:],
                                              hhi[:, bass.ds(GT * i, GT)].bitcast(F32), ALU.subtract).then_inc(hid_lo, 1)
                    product(p, up)
                    p = by_name[f"down{layer}{n}"]

                    if n == 0:
                        gate_ready(2 * layer + 1)
                        dve.wait_ge(ln_gb, 4 * (2 * layer + 1))
                    product(p, into_x)

            def into_x(i, g, units):
                dve.wait_ge(tile_used, units)
                for t in range(GT):
                    k = bass.ds(2 * GT * i + GT * g + t, 1)
                    last = dve.scalar_tensor_tensor(xT[:, k], pg[:, g % 2, t:t + 1], onep[:, 1, k], xT[:, k],
                                                    ALU.mult, ALU.add)
                last.then_inc(grp_done, 1)

            def gate_ready(n):
                gate, need = mod_cols(n)[2], mod_cols(n)[4]
                dve.wait_ge(mod_taken, need + 1)
                link(dve.tensor_scalar(onep[:, 1], mod[:, gate:gate + KT], 1.0, None, ALU.add))

            def split_h(n, q):
                for t in range(4 * q, 4 * q + 4):
                    last = dve.tensor_scalar(y[:, t], xT[:, t], fold[:, 0, t:t + 1], fold[:, 1, t:t + 1],
                                             ALU.mult, ALU.add)
                last.then_inc(h_ready, 1)
                k = slice(4 * q, 4 * q + 4)
                dve.wait_ge(h_ready, 4 * n + q + 1)
                dve.wait_ge(h_hi, 4 * n + q + 1)
                dve.tensor_tensor(alo[:, k], y[:, k], ahi[:, k].bitcast(F32), ALU.subtract).then_inc(act_ready, 1)

            def scale_ready(n):
                sh, sc, _, need, _ = mod_cols(n)
                dve.wait_ge(mod_taken, need + 1)
                link(dve.tensor_scalar(onep[:, 0], mod[:, sc:sc + KT], 1.0, None, ALU.add))
                return mod[:, sh:sh + KT]

            def layer_norm(n):
                dve.wait_ge(ln_mean, n + 1)
                for q in range(4):
                    k = slice(4 * q, 4 * q + 4)
                    dve.tensor_tensor(xT[:, k], xT[:, k], over(st[:, 0], 4), ALU.subtract).then_inc(ln_c, 1)
                if n < 3:
                    shift = scale_ready(n + 1)
                    c0 = (n % 2) * 2 * 32 + (n // 2) * KT
                    g, b = lnc[:, c0:c0 + KT], lnc[:, c0 + 32:c0 + 32 + KT]
                    dve.tensor_tensor(fold[:, 0], g, onep[:, 0], ALU.mult)
                    link(dve.tensor_tensor(fold[:, 1], b, onep[:, 0], ALU.mult))
                    dve.tensor_scalar(fold[:, 2], g, ALPHA, None, ALU.mult)
                    dve.tensor_scalar(fold[:, 3], b, ALPHA, None, ALU.mult)
                    link(dve.tensor_tensor(fold[:, 1], fold[:, 1], shift, ALU.add))
                dve.wait_ge(ln_c, 4 * n + 4)
                dve.wait_ge(ln_std, n + 1)
                link(dve.reciprocal(st[:, 1], st[:, 1]))
                for q in range(4):
                    k = slice(4 * q, 4 * q + 4)
                    dve.tensor_tensor(xT[:, k], xT[:, k], over(st[:, 1], 4), ALU.mult).then_inc(ln_n, 1)
                    if n < 3:
                        dve.wait_ge(ln_n, 4 * n + q + 1)
                        split_h(n + 1, q)

            dve.sem_inc(s5_read, 1)
            for steps in (s5gd, dnd, dnc, scd, dad):
                dve.sem_inc(steps.sem, steps.start)
            dve.sem_inc(lo_done, 4)
            dve.sem_inc(grp_done, 2)
            dve.sem_inc(ada_step, ADA_FREE)
            dve.sem_inc(mod_taken, 1)
            dve.memset(consts[:, 0:1], EPS)
            dve.memset(consts[:, 1:2], 1.5707962)
            dve.memset(consts[:, 3:4], 1e-6)
            dve.memset(consts[:, 4:5], 1.0).then_inc(vec_fix, 1)
            dve.wait_ge(vec_in, 16 * N_VEC_LOADS)
            dve.tensor_copy(vrow[64:96, 5].rearrange("p (g s) -> p g s", g=2),
                            vrow[64:96, 6, 0:2].unsqueeze(2).broadcast_to([32, 2, 64])).then_inc(vec_fix, 1)
            for n, (dst, bank, col, rows) in enumerate(VECS):
                dve.wait_ge(vec_turned, len(VECS))
                dve.tensor_copy(dst, bank[:, col:col + rows]).then_inc(vec_taken, 1)
            dve.wait_ge(c_tanh, 1)
            link(dve.scalar_tensor_tensor(cact[:], cact[:], 1.0, misc[:, 0:KT], ALU.add, ALU.mult))
            link(dve.tensor_scalar(cact[:], cact[:], 0.5, None, ALU.mult))

            are, aim = s5c[:, 0:32], s5c[:, 32:64]
            dve.wait_ge(s5_set.sem, s5_set.at(0, "delta"))
            dve.tensor_tensor(sv[:, 1], are, sv[:, 0], ALU.mult).then_inc(s5_setd.sem, 1)
            link(dve.scalar_tensor_tensor(sv[:, 3], aim, 1.0 / (2.0 * math.pi), sv[:, 0], ALU.mult, ALU.mult))
            link(dve.tensor_scalar(sv[:, 4], sv[:, 3], ROUND_1, ROUND_1, ALU.add, ALU.subtract))
            dve.tensor_tensor(sv[:, 4], sv[:, 3], sv[:, 4], ALU.subtract).then_inc(s5_setd.sem, 1)
            dve.wait_ge(s5_setd.sem, s5_setd.at(0, "f"))
            link(dve.tensor_copy(s5v[:, 0], sv[:, 4]))
            dve.wait_ge(s5_set.sem, s5_set.at(0, "sins"))
            link(dve.tensor_scalar(sv[:, 7], sv[:, 2], -1.0, 1.0, ALU.mult, ALU.add))
            link(dve.reciprocal(sv[:, 7], sv[:, 7]))
            link(dve.scalar_tensor_tensor(sv[:, 7], sv[:, 2], 2.0, sv[:, 7], ALU.mult, ALU.mult))
            link(dve.tensor_scalar(s5v[:, 2], sv[:, 7], 1.0, None, ALU.add))
            link(dve.scalar_tensor_tensor(sv[:, 8], sv[:, 6], -2.0, sv[:, 6], ALU.mult, ALU.mult))
            link(dve.scalar_tensor_tensor(sv[:, 9], sv[:, 8], 1.0, sv[:, 7], ALU.add, ALU.mult))
            link(dve.tensor_tensor(sv[:, 9], sv[:, 9], sv[:, 8], ALU.add))
            link(dve.tensor_tensor(sv[:, 10], s5v[:, 2], sv[:, 5], ALU.mult))
            link(dve.tensor_tensor(sv[:, 11], are, are, ALU.mult))
            link(dve.tensor_tensor(sv[:, 12], aim, aim, ALU.mult))
            link(dve.tensor_tensor(sv[:, 11], sv[:, 11], sv[:, 12], ALU.add))
            link(dve.reciprocal(sv[:, 11], sv[:, 11]))
            link(dve.tensor_tensor(sv[:, 12], sv[:, 9], are, ALU.mult))
            link(dve.tensor_tensor(sv[:, 13], sv[:, 10], aim, ALU.mult))
            link(dve.tensor_tensor(sv[:, 12], sv[:, 12], sv[:, 13], ALU.add))
            link(dve.tensor_tensor(sv[:, 12], sv[:, 12], sv[:, 11], ALU.mult))
            link(dve.tensor_tensor(sv[:, 13], sv[:, 10], are, ALU.mult))
            link(dve.tensor_tensor(sv[:, 14], sv[:, 9], aim, ALU.mult))
            link(dve.tensor_tensor(sv[:, 13], sv[:, 13], sv[:, 14], ALU.subtract))
            link(dve.tensor_tensor(sv[:, 13], sv[:, 13], sv[:, 11], ALU.mult))

            def ada_first(i):
                dve.wait_ge(ada_summed, 2 * i + 1)
                for j in range(4):
                    for b in range(2):
                        dve.wait_ge(ada_in_first[2 * j + b], 16 * i + 16)
                    for kk in range(UK):
                        for b in range(2):
                            n = 2 * (UK * j + kk) + b
                            unit, k = first_slots[2 * j + b][:, kk], UK * j + kk
                            if k == 0:
                                last = dve.tensor_scalar(acc[:, b], unit, cact[:, 0:1], None, ALU.mult)
                            else:
                                dve.wait_ge(ada_step, 32 * i + (n - 1 + ADA_FREE))
                                last = dve.scalar_tensor_tensor(acc[:, b], unit, cact[:, k:k + 1], acc[:, b],
                                                                ALU.mult, ALU.add)
                            last.then_inc(ada_step, 1)
                for b in range(2):
                    ada_take(2 * i + b)
            for n in range(8):
                dve.wait_ge(x_turned, n + 1)
                dve.tensor_scalar(xT[:, 2 * n:2 * n + 2], pgf[:, n % 4], ALPHA, None, ALU.mult).then_inc(x_taken, 1)
            bodies(dve, ADA_FIRST, ada_first)
            for j in (0, 1):
                dve.wait_ge(hi_done, j + 1)
                split_lo(j, j)
            shift = scale_ready(0)
            dve.tensor_scalar(fold[:, 0], onep[:, 0], 1.0 / ALPHA, None, ALU.mult)
            link(dve.tensor_copy(fold[:, 1], shift))
            dve.sem_inc(folded, 1)
            for q in range(4):
                split_h(0, q)
            fre, fim = along(sv[:, 12], 16), along(sv[:, 13], 16)
            b1, b2 = s5z[:].rearrange("p a l -> p (a l)").rearrange("p (t c) -> p t c", c=16), \
                s5m2[:].rearrange("p a l -> p (a l)").rearrange("p (t c) -> p t c", c=16)
            dve.wait_ge(par_in, 16 * N_PAR_LOADS)
            link(dve.tensor_tensor(b1, s5br[:], fim, ALU.mult))
            link(dve.tensor_tensor(b2, s5bi[:], fim, ALU.mult))
            link(dve.tensor_tensor(s5br[:], s5br[:], fre, ALU.mult))
            link(dve.tensor_tensor(s5br[:], s5br[:], b2, ALU.subtract))
            link(dve.tensor_tensor(s5bi[:], s5bi[:], fre, ALU.mult))
            dve.tensor_tensor(s5bi[:], s5bi[:], b1, ALU.add).then_inc(s5_setd.sem, 1)
            dve.sem_inc(s5d.sem, s5d.n)
            dve.wait_ge(s5_setp.sem, 1)

            product(by_name["in0u"], None, skip_last=True)
            dve.wait_ge(ba_done, 1)
            dve.tensor_copy(ba[:], pb[:, 0:2 * N_SMALL].rearrange("p (c n) -> p c n", c=2)).then_inc(ba_taken, 1)
            def s5_chain(i, j):
                n = 8 * i + j
                r = n + 1
                bu = pb[:].rearrange("p (a l) -> p a l", a=2)
                dve.wait_ge(s5a.sem, s5a.at(r, "tab2"))
                dve.wait_ge(s5_bu, n + 2)
                dve.wait_ge(s5_y, n + 1)
                dve.tensor_tensor(s5m1[:], bu, over(s5tab[:, 1], 2), ALU.mult).then_inc(s5d.sem, 1)
                dve.tensor_tensor(s5m2[:, 0], bu[:, 1], s5tab[:, 0], ALU.mult).then_inc(s5d.sem, 1)
                dve.tensor_tensor(s5m2[:, 1], bu[:, 0], s5tab[:, 2], ALU.mult).then_inc(s5d.sem, 1)
                dve.wait_ge(s5d.sem, s5d.at(r, "m2b"))
                dve.tensor_tensor(s5z[:], s5m1[:], s5m2[:], ALU.add).then_inc(s5d.sem, 1)
                dve.wait_ge(s5d.sem, s5d.at(r, "z"))
                decay = s5v[:, 2, bass.ds(n, 1)].broadcast_to([P, L])
                dve.tensor_tensor_scan(s5m1[:, 0], decay, s5z[:, 0], 0.0, ALU.mult, ALU.add).then_inc(s5d.sem, 1)
                dve.tensor_tensor_scan(s5m1[:, 1], decay, s5z[:, 1], 0.0, ALU.mult, ALU.add).then_inc(s5d.sem, 1)
                dve.wait_ge(s5d.sem, s5d.at(r, "si"))
                dve.tensor_tensor(s5m2[:], s5m1[:], s5tab[:, 1:3], ALU.mult).then_inc(s5d.sem, 1)
                dve.tensor_tensor(s5z[:], s5m1[:], s5tab[:, 0:2], ALU.mult).then_inc(s5d.sem, 1)
                dve.wait_ge(s5d.sem, s5d.at(r, "p2"))
                dve.tensor_tensor(s5m1[:, 0], s5m2[:, 0], s5m2[:, 1], ALU.add).then_inc(s5d.sem, 1)
                dve.tensor_tensor(s5m1[:, 1], s5z[:, 0], s5z[:, 1], ALU.add).then_inc(s5d.sem, 1)

            def s5_gelu(t, parts):
                def step(name, ins):
                    ins.then_inc(s5gd.sem, 1)
                    dve.wait_ge(s5gd.sem, s5gd.at(t, name))

                yt = pr[:, bass.ds(t, 1)]
                if 0 in parts:
                    dve.wait_ge(s5_y, 4 * t + 5)
                    dve.scalar_tensor_tensor(yt, yt, misc[:, bass.ds(40 + t, 1)], pc[:, 0:L].unsqueeze(1),
                                             ALU.mult, ALU.add).then_inc(s5_read, 1)
                    dve.wait_ge(s5_read, t + 2)
                if 1 in parts:
                    step("y2", dve.tensor_tensor(s5g[:], yt, yt, ALU.mult))
                    step("p", dve.tensor_scalar(s5g[:], s5g[:], 0.044715, 1.0, ALU.mult, ALU.add))
                    dve.tensor_tensor(s5g[:], s5g[:], yt, ALU.mult).then_inc(s5gd.sem, 1)
                if 2 in parts:
                    dve.wait_ge(s5ga.sem, s5ga.at(t, "th"))
                    step("s", dve.scalar_tensor_tensor(s5g[:], s5g[:], 1.0, yt, ALU.add, ALU.mult))
                    dve.tensor_scalar(yt, s5g[:], 0.5, None, ALU.mult).then_inc(s5gd.sem, 1)

            def s5_after(i, j):
                first, second = 2 * i, 2 * i + 1
                {3: lambda: s5_gelu(first, (0,)), 4: lambda: s5_gelu(first, (1,)), 5: lambda: s5_gelu(first, (2,)),
                 7: lambda: s5_gelu(second, (0, 1, 2))}.get(j, lambda: None)()

            product(by_name["in0"], None, s5_chain, s5_after, lag=1)
            for q in range(2):
                dve.wait_ge(s5_hi, q + 1)
                dve.tensor_tensor(alo[:, 4 * q:4 * q + 4], pr[:, 4 * q:4 * q + 4],
                                  ahi[:, 4 * q:4 * q + 4].bitcast(F32), ALU.subtract).then_inc(s5_lo, 1)
            dve.wait_ge(hi_done, by_name["glu"]["u0"] + 2)
            split_lo(1, 1)

            def glu(i, g, units):
                k = slice(GT * g, GT * g + GT)
                dve.wait_ge(glu_t, g + 1)
                dve.scalar_tensor_tensor(pr[:, k], pg[:, g], 1.0, pr[:, k], ALU.add, ALU.mult).then_inc(glu_s, 1)
                dve.wait_ge(glu_hi, g + 1)
                k2 = slice(HT + GT * g, HT + GT * g + GT)
                dve.scalar_tensor_tensor(alo[:, k2], pr[:, k], 0.5, ahi[:, k2].bitcast(F32), ALU.mult,
                                         ALU.subtract).then_inc(grp_done, 1)
            product(by_name["glu"], glu)
            deltanet_dve(dve, link, ada_unit, ada_take)
            gate_ready(0)
            product(by_name["out0"], into_x)
            layer_norm(0)
            ffn(0)
            layer_norm(1)
            def late_conv(i, j):
                if j in (0, 3, 4, 7):
                    if j == 0:
                        dve.wait_ge(grp_done, by_name["in1"]["g0"] + 6 + 2)
                    short_conv(dve, 4 * i + (0, 3, 4, 7).index(j))
            product(by_name["in1"], None, late=late_conv)
            attention_dve(dve)
            gate_ready(2)
            dve.wait_ge(ln_gb, 8)
            product(by_name["out1"], into_x)
            layer_norm(2)
            ffn(1)
            layer_norm(3)
            for n in range(8):
                dve.wait_ge(o_turned, n + 1)
                dve.tensor_copy(orow[:, n // 4, GROUP * (n % 4):GROUP * (n % 4 + 1)], pgf[:, n % 4]).then_inc(o_taken, 1)

        @block.tensor
        def _(pe):
            def ada_sum(ab, b, done=None):
                pe.wait_ge(ada_step, 16 * (ab + 1 if done is None else done) + ADA_FREE)
                pe.wait_ge(mod_taken, ab + 1)
                for t in range(GT):
                    last = pe.matmul(pm[:, t:t + 1], acc[:, b, P * t:P * t + P], ones[:, 0:1], start=True, stop=True)
                last.then_inc(ada_summed, 1)

            def product(p, ready, hi=None, lo=None, mid=None, after=None):
                hi, lo = hi if hi is not None else ahi, lo if lo is not None else alo

                def body(i):
                    for j in range(p["bu"]):
                        u = p["u0"] + p["bu"] * i + j
                        g, q = j // p["units"], j % p["units"]
                        pe.wait_ge(lo_done, u + 5)
                        ready(q)
                        if q == 0:
                            pe.wait_ge(grp_done, p["g0"] + p["bg"] * i + g + 1)
                        for kk in range(UK):
                            k = UK * q + kk
                            if mid and kk == UK // 2:
                                mid(i, j)
                            for n in range(GT):
                                dst, cols = pg[:, g % 2, n], slice(P * n, P * n + P)
                                pe.matmul(dst, whi[:, j % 2, kk, cols], hi[:, k], start=(k == 0 and n % 2 == 0),
                                          stop=False, skip_group_check=True)
                                pe.matmul(dst, whi[:, j % 2, kk, cols], lo[:, k], start=False,
                                          stop=False, skip_group_check=True)
                                last = pe.matmul(dst, wlo[:, j % 2, kk, cols], hi[:, k], start=False,
                                                 stop=(k == UK * p["units"] - 1), skip_group_check=True)
                        last.then_inc(tile_used, 1)
                        if j in p["sums"]:
                            b = p["sums"][j]
                            ada_sum(p["ab0"] + b + p["ada"] * i, b)
                        if after:
                            after(i, j)
                bodies(pe, p["bodies"], body, peel=after is not None)

            def on_act(n):
                return lambda q: pe.wait_ge(act_ready, 4 * n + q + 1)

            def ffn(layer):
                for n, (first, groups) in enumerate(FFN_BLOCKS):
                    product(by_name[f"up{layer}{n}"], on_act(2 * layer + 1))
                    product(by_name[f"down{layer}{n}"],
                            lambda q, done=FFN_GROUPS * layer + first: pe.wait_ge(hid_lo, done + q + 1), hhi, hlo)

            def layer_norm(n, p):
                groups = p["g0"] + p["bodies"] * p["bg"]
                for k in range(KT):
                    if k % 4 == 0:
                        pe.wait_ge(grp_done, groups - 4 + k // 4 + 1 + 2)
                    last = pe.matmul(pa[:, 0:L], ones[:], xT[:, k], start=(k == 0), stop=(k == KT - 1))
                last.then_inc(ln_sum, 1)
                for k in range(KT):
                    if k % 4 == 0:
                        pe.wait_ge(ln_sq, 4 * n + k // 4 + 1)
                    last = pe.matmul(pb[:, 0:L], ones[:], y[:, k], start=(k == 0), stop=(k == KT - 1))
                last.then_inc(ln_var, 1)

            pe.sem_inc(ada_summed, 1)
            for steps in (s5_turned, s5_bu, s5_y):
                pe.sem_inc(steps, 1)
            for steps in (dne, dae_):
                pe.sem_inc(steps.sem, steps.start)
            pe.wait_ge(const_done, 1)
            pe.wait_ge(vec_in, 16 * N_VEC_LOADS)
            pe.wait_ge(vec_fix, 2)
            for n, (_, bank, col, rows) in enumerate(VECS):
                pe.transpose(bank[:, col:col + rows], vrow[0:rows, n], ident[0:rows, 0:rows]).then_inc(vec_turned, 1)
            pe.wait_ge(x_in, 16)
            for n in range(8):
                if n >= 4:
                    pe.wait_ge(x_taken, n - 3)
                for t in range(2):
                    for b in range(2):
                        f = 2 * n + t
                        last = pe.transpose(pgf[:, n % 4, L * t + P * b:L * t + P * b + P], xrow[:, b, P * f:P * f + P],
                                            ident[:])
                last.then_inc(x_turned, 1)

            def ada_first(i):
                for b in range(2):
                    ada_sum(2 * i + b, b, 2 * i + 2)
            bodies(pe, ADA_FIRST, ada_first)
            pe.wait_ge(x_taken, 8)
            def logits(i, j):
                if j != 1:
                    return
                pe.wait_ge(par_in, 16 * N_PAR_LOADS)
                for b in range(2):
                    for k in range(KT):
                        if b == 0 and k % 4 == 0:
                            pe.wait_ge(h_ready, k // 4 + 1)
                        last = pe.matmul(pb[:, N_SMALL * b:N_SMALL * b + N_SMALL], y[:, k, P * b:P * b + P],
                                         wba[:, k], start=(k == 0), stop=(k == KT - 1))
                last.then_inc(ba_done, 1)
            product(by_name["in0u"], on_act(0), after=logits)
            pe.wait_ge(ba_taken, 1)
            pe.wait_ge(grp_done, by_name["in0"]["g0"] + 2)

            def s5_turn(n):
                pe.wait_ge(s5p.sem, s5p.at(n + 1, "pad"))
                pe.wait_ge(s5a.sem, s5a.at(n, "wneg"))
                for m in range(4):
                    last = pe.transpose(pa[:, P * m:P * m + P], s5pad[:, m], ident[:])
                last.then_inc(s5_turned, 1)

            def s5_in(n, t):
                pe.wait_ge(s5a.sem, s5a.at(n + 1, "wb"))
                pe.wait_ge(s5d.sem, s5d.at(n, "m2b"))
                for m in range(2):
                    last = pe.matmul(pb[:, L * m:L * m + L], s5w[:, m], pr[:, bass.ds(t, 1)], start=True, stop=True)
                last.then_inc(s5_bu, 1)

            def s5_out(n, t, s):
                if s == 0:
                    pe.wait_ge(s5_read, t + 1)
                pe.wait_ge(s5d.sem, s5d.at(n + 1, "q2"))
                pe.wait_ge(s5a.sem, s5a.at(n + 1, "wneg"))
                for m in range(2):
                    last = pe.matmul(pc[:, 0:L], s5w[:, 2 + m], s5m1[:, m], start=(s == 0 and m == 0),
                                     stop=(s == 3 and m == 1))
                last.then_inc(s5_y, 1)

            def s5_mid(i, j):
                n = 8 * i + j + 1
                if not (isinstance(n, int) and n == S5_TILES):
                    s5_turn(n)

            def s5_after(i, j):
                n = 8 * i + j
                s5_out(n, 2 * i + j // 4, j % 4)
                if not (isinstance(n, int) and n == S5_TILES - 1):
                    s5_in(n + 1, 2 * i + (j + 1) // 4)

            s5_turn(0)
            s5_in(0, 0)
            product(by_name["in0"], on_act(0), mid=s5_mid, after=s5_after)
            product(by_name["glu"], lambda q: pe.wait_ge(s5_lo, q + 1))
            deltanet_pe(pe, ada_sum)
            product(by_name["out0"], lambda q: pe.wait_ge(dnd.sem, dnd.at(3, "lo")))
            layer_norm(0, by_name["out0"])
            ffn(0)
            layer_norm(1, by_name["down02"])
            product(by_name["in1"], on_act(2))
            attention_pe(pe)
            product(by_name["out1"], lambda q: pe.wait_ge(sc_lo, q + 1) if q < 2 else
                    pe.wait_ge(dad.sem, dad.at(2 * q - 3, "lo")))
            layer_norm(2, by_name["out1"])
            ffn(1)
            layer_norm(3, by_name["down12"])
            for n in range(8):
                b, q = n // 4, n % 4
                pe.wait_ge(ln_gb, 4 * 3 + q + 1)
                if n >= 4:
                    pe.wait_ge(o_taken, n - 3)
                for t in range(4):
                    last = pe.transpose(pgf[:, n % 4, P * t:P * t + P], xT[:, 4 * q + t, P * b:P * b + P], ident[:])
                last.then_inc(o_turned, 1)

        @block.gpsimd
        def _(pool):
            def load_product(p):
                def body(i, start=0):
                    src, col0 = ada_source(p["ab0"] + start * p["ada"])
                    col0 -= start * p["ada"] * GROUP
                    for n in range(4 * p["ada"]):
                        ab = n // 4 + p["ada"] * i
                        load_ada(pool, ada_in_pool, src, col0 + GROUP * ab, p["ab0"] + ab, n % 4)
                if p["ab0"] < LAYER_BLOCKS < p["ab0"] + p["bodies"] * p["ada"]:
                    start = (LAYER_BLOCKS - p["ab0"]) // p["ada"]
                    bodies(pool, start, body)
                    bodies(pool, p["bodies"] - start, lambda i: body(i + start, start=start))
                elif p["ada"]:
                    bodies(pool, p["bodies"], body)

            pool.sem_inc(dnp.sem, dnp.start)
            pool.memset(pidle[:], 0.0)
            pool.memset(ones[:], 1.0)
            pool.memset(ident[:], 0.0).then_inc(pool_c, 1)
            pool.wait_ge(pool_c, 1)
            pool.affine_select(out=ident[:], in_=ident[:], compare_op=ALU.not_equal, fill=1.0, base=0,
                               pattern=[[-1, P]], channel_multiplier=1).then_inc(const_done, 1)
            for s in range(4):
                pool.memset(s5mk[:, s], 1.0)
                pool.memset(s5mt[:, s], 1.0)
            pool.iota(tcol[:], [[1, L]], base=-L // 2, channel_multiplier=0, allow_small_or_imprecise_dtypes=True).then_inc(pool_c, 1)
            pool.wait_ge(pool_c, 2)
            for s in range(4):
                for h in range(2):
                    g = 2 * s + h
                    v = s5mk[:, s, 64 * h:64 * h + 64]
                    link_pool(pool, pool.affine_select(out=v, in_=v, compare_op=ALU.is_ge, fill=0.0, base=-16 * g,
                                                       pattern=[[0, 64]], channel_multiplier=1))
                    link_pool(pool, pool.affine_select(out=v, in_=v, compare_op=ALU.is_ge, fill=0.0, base=16 * g + 15,
                                                       pattern=[[0, 64]], channel_multiplier=-1))
                v = s5mt[:, s]
                for h in range(8):
                    w = v[:, 16 * h:16 * h + 16]
                    if h == 2 * s:
                        ok = dict(compare_op=ALU.is_ge, base=63, channel_multiplier=-1)
                    elif h == 2 * s + 1:
                        ok = dict(compare_op=ALU.is_ge, base=-64, channel_multiplier=1)
                    else:
                        ok = dict(compare_op=ALU.is_ge, base=-1, channel_multiplier=0)
                    link_pool(pool, pool.affine_select(out=w, in_=w, fill=0.0, pattern=[[0, 16]], **ok))
            pool.sem_inc(s5_setp.sem, 1)
            load_product(by_name["in0u"])
            pool.wait_ge(s5_setd.sem, s5_setd.at(0, "done"))
            pool.sem_inc(s5p.sem, s5p.n)
            with pool.Fori(0, HT) as t:
                for s in range(4):
                    i = 4 * t + s + 1
                    pool.wait_ge(s5_turned, i)
                    for n, src in enumerate((s5br, s5bi)):
                        pool.tensor_tensor(s5pad[:, n].rearrange("p (h c) -> p h c", c=16),
                                           src[:, bass.ds(4 * t + s, 1)].broadcast_to([P, 8, 16]),
                                           s5mt[:, s].rearrange("p (h c) -> p h c", c=16), ALU.mult)
                    for n, src in enumerate((s5cr, s5ci)):
                        last = pool.tensor_tensor(s5pad[:, 2 + n].rearrange("p (h c) -> p h c", c=64),
                                                  src[:, bass.ds(t, 1)].broadcast_to([P, 2, 64]),
                                                  s5mk[:, s].rearrange("p (h c) -> p h c", c=64), ALU.mult)
                    last.then_inc(s5p.sem, 1)
                    k = 4 * t + s
                    a0, a1 = s5arg[:, 0], s5arg[:, 1]
                    pool.wait_ge(s5a.sem, s5a.at(i - 1, "tab2"))
                    pool.tensor_tensor(a0, tcol[:], s5v[:, 0, bass.ds(k, 1)].broadcast_to([P, L]), ALU.mult).then_inc(s5p.sem, 1)
                    pool.wait_ge(s5p.sem, s5p.at(i, "turns"))
                    carry(pool)
                    pool.tensor_scalar(a1, a0, ROUND_1, ROUND_1, ALU.add, ALU.subtract).then_inc(s5p.sem, 1)
                    pool.wait_ge(s5p.sem, s5p.at(i, "whole"))
                    pool.tensor_tensor(a0, a0, a1, ALU.subtract).then_inc(s5p.sem, 1)
                    pool.wait_ge(s5p.sem, s5p.at(i, "sine"))
                    carry(pool)
                    pool.tensor_scalar(a1, a0, 0.25, -1.0, ALU.is_gt, ALU.mult).then_inc(s5p.sem, 1)
                    pool.wait_ge(s5p.sem, s5p.at(i, "over"))
                    pool.tensor_tensor(a1, a0, a1, ALU.add).then_inc(s5p.sem, 1)
            deltanet_pool(pool)
            load_product(by_name["out0"])
            for p in products:
                if p["name"][:-1] in ("up0", "down0"):
                    load_product(p)
            attention_pool(pool)
            load_product(by_name["in1"])
            load_product(by_name["out1"])
            load_product(by_name["up10"])


_INS = ['x', 'c', 'ada_w', 'ada_b', 'ln1_g', 'ln1_b', 'ln2_g', 'ln2_b', 'ffn_w_gate', 'ffn_w_up', 'ffn_w_down',
        'ab_w_in', 'ab_w_out', 'dn_conv_w', 'dn_a_log', 'dn_dt_bias', 'dn_norm_g',
        's5_a_re', 's5_a_im', 's5_b_re', 's5_b_im', 's5_c_re', 's5_c_im', 's5_d', 's5_log_dt', 's5_w_glu',
        'cd_w_in', 'cd_w_out', 'sc_conv_w', 'da_lq1', 'da_lk1', 'da_lq2', 'da_lk2', 'da_norm_g']
_OUTS = [((1, 256, 2048), 'float32')]


def kernel(**inputs):
    import numpy as _np
    import concourse.bacc as _bacc
    from concourse import mybir as _mybir
    from concourse.bass_utils import run_bass_kernel_spmd as _run

    nc = _bacc.Bacc("TRN2", target_bir_lowering=False, num_devices=1)
    arrays, args = {}, []
    for name in _INS:
        a = _np.ascontiguousarray(inputs[name])
        arrays[f"in_{name}_dram"] = a
        args.append(nc.dram_tensor(f"in_{name}_dram", a.shape, _mybir.dt.from_np(a.dtype), kind="ExternalInput").ap())
    for i, (shape, dtype) in enumerate(_OUTS):
        dt = _mybir.dt.from_np(_np.dtype(dtype))
        args.append(nc.dram_tensor(f"out_{i}_dram", shape, dt, kind="ExternalOutput").ap())
    build(nc, *args)
    r = _run(nc, [arrays], core_ids=[0])
    got = tuple(r.results[0][f"out_{i}_dram"] for i in range(len(_OUTS)))
    return got[0]
```
